# Optimizing a Trainium2 kernel written in Bass

```python
import math
import jax
import jax.numpy as jnp
from jax import lax
import numpy as np
import jax, jax.numpy as jnp

D_MODEL = 1024
BATCH = 1
SEQ = 512
DEPTH = 2

N_MIXERS = 4
EXPAND = 2
D_INNER = EXPAND * D_MODEL
EPS = 1e-6

SSD_HEAD_DIM = 64
SSD_HEADS = D_INNER // SSD_HEAD_DIM
SSD_GROUPS = 8
SSD_HPG = SSD_HEADS // SSD_GROUPS
SSD_STATE = 128
SSD_CONV = 5
SSD_CHUNK = 128
SSD_CONV_DIM = D_INNER + 2 * SSD_GROUPS * SSD_STATE
SSD_PROJ = D_INNER + SSD_CONV_DIM + 2 * SSD_HEADS

GLA_HEADS = 4
GLA_DK = D_MODEL // 2 // GLA_HEADS
GLA_DV = D_INNER // GLA_HEADS
GLA_RANK = 16
GLA_NORMALIZER = 16.0
GLA_CHUNK = 64
GLA_QK = GLA_HEADS * GLA_DK
GLA_PROJ = 2 * GLA_QK + 2 * D_INNER + 2 * GLA_RANK

HY_ORDER = 2
HY_SHORT = 3
HY_EMB = 33
HY_BANDS = (HY_EMB - 1) // 2
HY_FFN = 64
HY_INNER = 2
HY_FAST_PCT = 0.3
HY_SLOW_PCT = 1.5
HY_TARGET = 1e-2
HY_PROJ = (HY_ORDER + 2) * D_INNER
HY_FILT = 2 * HY_ORDER * D_INNER

ML_HEADS = 4
ML_DH = D_INNER // ML_HEADS
ML_DK = ML_DH // 2
ML_CONV = 5
ML_CHUNK = 64
ML_PROJ = 3 * D_INNER + 4 * ML_HEADS


def rmsnorm(x, g):
    xf = x.astype(jnp.float32)
    y = xf * lax.rsqrt(jnp.mean(xf * xf, axis=-1, keepdims=True) + EPS)
    return (y * g.astype(jnp.float32)).astype(x.dtype)

def dwconv(x, w, b):
    k = w.shape[0]
    y = lax.conv_general_dilated(x, w[:, None, :].astype(x.dtype), (1,), [((k - 1) // 2, (k - 1) // 2)],
                                 dimension_numbers=('NWC', 'WIO', 'NWC'), feature_group_count=x.shape[-1])
    return y + b.astype(x.dtype)

def rev(t):
    return jnp.flip(t, axis=1)

def to_chunks(t, q):
    b, l = t.shape[0], t.shape[1]
    return jnp.moveaxis(t.reshape((b, l // q, q) + t.shape[2:]), 1, 0)

def from_chunks(t):
    t = jnp.moveaxis(t, 0, 1)
    return t.reshape((t.shape[0], t.shape[1] * t.shape[2]) + t.shape[3:])

def ssd_scan(xh, dt, a, bm, cm):
    bsz, seq = xh.shape[:2]
    grp = (SSD_GROUPS, SSD_HPG)
    xs = to_chunks(xh.reshape((bsz, seq) + grp + (SSD_HEAD_DIM,)), SSD_CHUNK)
    dts = to_chunks(dt.reshape((bsz, seq) + grp), SSD_CHUNK)
    las = to_chunks((dt * a).reshape((bsz, seq) + grp), SSD_CHUNK)
    bs = to_chunks(bm, SSD_CHUNK)
    cs = to_chunks(cm, SSD_CHUNK)
    causal = jnp.tril(jnp.ones((SSD_CHUNK, SSD_CHUNK), bool))[None, :, :, None, None]

    def step(state, inp):
        xc, dtc, lac, bc, cc = inp
        cum = jnp.cumsum(lac, axis=1)
        decay = jnp.exp(jnp.where(causal, cum[:, :, None] - cum[:, None], -jnp.inf))
        xdt = xc * dtc[..., None]
        cb = jnp.einsum('blgn,bsgn->blsg', cc, bc)
        y = jnp.einsum('blsgr,bsgrp->blgrp', cb[..., None] * decay, xdt)
        y = y + jnp.einsum('blgn,bgrpn->blgrp', cc, state) * jnp.exp(cum)[..., None]
        tail = jnp.exp(cum[:, -1:] - cum)
        state = (state * jnp.exp(cum[:, -1])[..., None, None]
                 + jnp.einsum('bsgn,bsgrp->bgrpn', bc, xdt * tail[..., None]))
        return state, y

    state0 = jnp.zeros((bsz,) + grp + (SSD_HEAD_DIM, SSD_STATE), jnp.float32)
    _, ys = lax.scan(step, state0, (xs, dts, las, bs, cs))
    return from_chunks(ys).reshape(xh.shape)

def ssd_mixer(u, w_in, conv_w, conv_b, dt_bias, a_log, d_skip, gnorm, w_out):
    f32 = jnp.float32
    bsz, seq = u.shape[:2]
    z, xbc, dt = jnp.split(u @ w_in, [D_INNER, D_INNER + SSD_CONV_DIM], axis=-1)
    xbc = jax.nn.silu(dwconv(xbc, conv_w, conv_b)).astype(f32)
    xh, bm, cm = jnp.split(xbc, [D_INNER, D_INNER + SSD_GROUPS * SSD_STATE], axis=-1)
    xh = xh.reshape(bsz, seq, SSD_HEADS, SSD_HEAD_DIM)
    bm = bm.reshape(bsz, seq, SSD_GROUPS, SSD_STATE)
    cm = cm.reshape(bsz, seq, SSD_GROUPS, SSD_STATE)
    dt = jax.nn.softplus(dt.astype(f32).reshape(bsz, seq, 2, SSD_HEADS) + dt_bias.astype(f32))
    a = -jnp.exp(a_log.astype(f32))
    y = (ssd_scan(xh, dt[:, :, 0], a[0], bm, cm)
         + rev(ssd_scan(rev(xh), rev(dt[:, :, 1]), a[1], rev(bm), rev(cm)))
         + xh * d_skip.astype(f32)[:, None])
    y = y.reshape(bsz, seq, D_INNER) * jax.nn.silu(z.astype(f32))
    y = rmsnorm(y.reshape(bsz, seq, SSD_GROUPS, D_INNER // SSD_GROUPS), gnorm.reshape(SSD_GROUPS, -1))
    return y.reshape(bsz, seq, D_INNER).astype(u.dtype) @ w_out

def gla_scan(q, k, v, lg):
    bsz = q.shape[0]
    causal = jnp.tril(jnp.ones((GLA_CHUNK, GLA_CHUNK), bool))[None, None]

    def step(s, inp):
        qc, kc, vc, gc = inp
        cum = jnp.cumsum(gc, axis=1)
        qg = qc * jnp.exp(cum)
        kg = kc * jnp.exp(-cum)
        att = jnp.where(causal, jnp.einsum('blhk,bshk->bhls', qg, kg), 0.0)
        o = jnp.einsum('bhls,bshv->blhv', att, vc) + jnp.einsum('blhk,bhkv->blhv', qg, s)
        kd = kc * jnp.exp(cum[:, -1:] - cum)
        s = s * jnp.exp(cum[:, -1])[..., None] + jnp.einsum('bshk,bshv->bhkv', kd, vc)
        return s, o

    s0 = jnp.zeros((bsz, GLA_HEADS, GLA_DK, GLA_DV), jnp.float32)
    _, os_ = lax.scan(step, s0, tuple(to_chunks(t, GLA_CHUNK) for t in (q, k, v, lg)))
    return from_chunks(os_)

def gla_mixer(u, w_in, w_gate, b_gate, onorm, w_out):
    f32 = jnp.float32
    bsz, seq = u.shape[:2]
    q, k, v, z, gl = jnp.split(u @ w_in, [GLA_QK, 2 * GLA_QK, 2 * GLA_QK + D_INNER, 2 * GLA_QK + 2 * D_INNER], axis=-1)
    q = q.astype(f32).reshape(bsz, seq, GLA_HEADS, GLA_DK) * (GLA_DK ** -0.5)
    k = k.astype(f32).reshape(bsz, seq, GLA_HEADS, GLA_DK)
    v = v.astype(f32).reshape(bsz, seq, GLA_HEADS, GLA_DV)
    gl = gl.astype(f32).reshape(bsz, seq, 2, GLA_RANK)
    lg = jax.nn.log_sigmoid(jnp.einsum('bldr,drk->bldk', gl, w_gate.astype(f32)) + b_gate.astype(f32)) / GLA_NORMALIZER
    lg = lg.reshape(bsz, seq, 2, GLA_HEADS, GLA_DK)
    o = gla_scan(q, k, v, lg[:, :, 0]) + rev(gla_scan(rev(q), rev(k), rev(v), rev(lg[:, :, 1])))
    o = rmsnorm(o, onorm).reshape(bsz, seq, D_INNER) * jax.nn.silu(z.astype(f32))
    return o.astype(u.dtype) @ w_out

def hyena_filters(seq_len, w_in, b_in, w_hid, b_hid, freq, w_out):
    f32 = jnp.float32
    t = jnp.linspace(0.0, 1.0, seq_len, dtype=f32)[:, None]
    pos = jnp.arange(seq_len, dtype=f32)[:, None]
    bands = jnp.linspace(1e-4, HY_BANDS - 1, HY_BANDS, dtype=f32)[None]
    ang = (2.0 * math.pi / seq_len) * pos * bands
    feats = jnp.concatenate([t, jnp.cos(ang), -jnp.sin(ang)], axis=-1)
    freq = freq.astype(f32)
    h = jnp.sin(freq[0] * (feats @ w_in.astype(f32) + b_in.astype(f32)))
    for j in range(HY_INNER):
        h = jnp.sin(freq[j + 1] * (h @ w_hid[j].astype(f32) + b_hid[j].astype(f32)))
    h = (h @ w_out.astype(f32)).reshape(seq_len, 2, HY_ORDER, D_INNER)
    max_decay = math.log(HY_TARGET) / HY_FAST_PCT
    min_decay = math.log(HY_TARGET) / HY_SLOW_PCT
    deltas = jnp.abs(jnp.linspace(min_decay, max_decay, D_INNER, dtype=f32))
    return h * jnp.exp(-t[:, :, None, None] * deltas)

def long_conv(y, h_f, h_b):
    seq = y.shape[1]
    k = jnp.concatenate([h_f, jnp.zeros_like(h_f[:1]), jnp.flip(h_b[1:], axis=0)], axis=0)
    yf = jnp.fft.rfft(y, n=2 * seq, axis=1)
    kf = jnp.fft.rfft(k, axis=0)
    return jnp.fft.irfft(yf * kf[None], n=2 * seq, axis=1)[:, :seq]

def hyena_mixer(u, w_in, conv_w, conv_b, ffn_w_in, ffn_b_in, ffn_w_hid, ffn_b_hid, ffn_freq, ffn_w_out, d_bias, w_out):
    f32 = jnp.float32
    seq = u.shape[1]
    proj = u @ w_in
    sig = dwconv(proj[..., :3 * D_INNER], conv_w, conv_b).astype(f32)
    z = proj[..., 3 * D_INNER:]
    v, x1, x2 = jnp.split(sig, 3, axis=-1)
    filt = hyena_filters(seq, ffn_w_in, ffn_b_in, ffn_w_hid, ffn_b_hid, ffn_freq, ffn_w_out)
    d_bias = d_bias.astype(f32)
    y = v
    for o, gate in enumerate((x1, x2)):
        y = gate * (long_conv(y, filt[:, 0, o], filt[:, 1, o]) + y * d_bias[o])
    y = y * jax.nn.silu(z.astype(f32))
    return y.astype(u.dtype) @ w_out

def mlstm_scan(q, k, v, li, lf):
    bsz = q.shape[0]
    causal = jnp.tril(jnp.ones((ML_CHUNK, ML_CHUNK), bool))[None, :, :, None]

    def step(carry, inp):
        c, n, m = carry
        qc, kc, vc, ic, fc = inp
        b = jnp.cumsum(fc, axis=1)
        logd = jnp.where(causal, b[:, :, None] - b[:, None] + ic[:, None], -jnp.inf)
        inter = b + m[:, None]
        m_row = jnp.maximum(jnp.max(logd, axis=2), inter)
        s = jnp.einsum('blhk,bshk->blsh', qc, kc) * jnp.exp(logd - m_row[:, :, None])
        scale = jnp.exp(inter - m_row)
        num = jnp.einsum('blsh,bshv->blhv', s, vc) + jnp.einsum('blhk,bhkv->blhv', qc, c) * scale[..., None]
        den = jnp.sum(s, axis=2) + jnp.einsum('blhk,bhk->blh', qc, n) * scale
        hc = num / jnp.maximum(jnp.abs(den), jnp.exp(-m_row))[..., None]
        tot = b[:, -1]
        lw = tot[:, None] - b + ic
        m_new = jnp.maximum(tot + m, jnp.max(lw, axis=1))
        w = jnp.exp(lw - m_new[:, None])
        dec = jnp.exp(tot + m - m_new)
        c = c * dec[..., None, None] + jnp.einsum('bsh,bshk,bshv->bhkv', w, kc, vc)
        n = n * dec[..., None] + jnp.einsum('bsh,bshk->bhk', w, kc)
        return (c, n, m_new), hc

    carry0 = (jnp.zeros((bsz, ML_HEADS, ML_DK, ML_DH), jnp.float32),
              jnp.zeros((bsz, ML_HEADS, ML_DK), jnp.float32),
              jnp.full((bsz, ML_HEADS), -jnp.inf, jnp.float32))
    _, hs = lax.scan(step, carry0, tuple(to_chunks(t, ML_CHUNK) for t in (q, k, v, li, lf)))
    return from_chunks(hs)

def mlstm_mixer(u, w_in, conv_w, conv_b, w_q, w_k, w_v, gate_b, skip, onorm, w_out):
    f32 = jnp.float32
    bsz, seq = u.shape[:2]
    xm, z, og, gates = jnp.split(u @ w_in, [D_INNER, 2 * D_INNER, 3 * D_INNER], axis=-1)
    ch = jax.nn.silu(dwconv(xm, conv_w, conv_b)).astype(f32).reshape(bsz, seq, ML_HEADS, ML_DH)
    xmh = xm.astype(f32).reshape(bsz, seq, ML_HEADS, ML_DH)
    q = jnp.einsum('blhd,hdk->blhk', ch, w_q.astype(f32))
    k = jnp.einsum('blhd,hdk->blhk', ch, w_k.astype(f32)) * (ML_DK ** -0.5)
    v = jnp.einsum('blhd,hde->blhe', xmh, w_v.astype(f32))
    g = gates.astype(f32).reshape(bsz, seq, 2, 2, ML_HEADS) + gate_b.astype(f32)
    li = g[:, :, :, 0]
    lf = jax.nn.log_sigmoid(g[:, :, :, 1])
    h = (mlstm_scan(q, k, v, li[:, :, 0], lf[:, :, 0])
         + rev(mlstm_scan(rev(q), rev(k), rev(v), rev(li[:, :, 1]), rev(lf[:, :, 1]))))
    h = jax.nn.sigmoid(og.astype(f32)).reshape(bsz, seq, ML_HEADS, ML_DH) * h
    h = rmsnorm(h, onorm) + skip.astype(f32) * ch
    h = h.reshape(bsz, seq, D_INNER) * jax.nn.silu(z.astype(f32))
    return h.astype(u.dtype) @ w_out

def first_inputs(seed: int = 0) -> dict:
    key = jax.random.key(seed)
    keys = iter(jax.random.split(key, 64))
    f32 = jnp.float32

    def nrm(shape, scale):
        return scale * jax.random.normal(next(keys), shape, f32)

    def gain(shape):
        return 1.0 + nrm(shape, 0.02)

    na, nb, nh, nm = (len(range(t, DEPTH, N_MIXERS)) for t in range(N_MIXERS))
    w_in_s = D_MODEL ** -0.5
    w_out_s = D_INNER ** -0.5
    x = nrm((BATCH, SEQ, D_MODEL), 1.0)
    dt0 = jnp.exp(jax.random.uniform(next(keys), (na, 2, SSD_HEADS), f32, math.log(1e-3), math.log(1e-1)))
    ssd_dt_bias = dt0 + jnp.log(-jnp.expm1(-dt0))
    ssd_a_log = jnp.log(jax.random.uniform(next(keys), (na, 2, SSD_HEADS), f32, 1.0, 16.0))
    ml_gate_b = jnp.concatenate([nrm((nm, 2, 1, ML_HEADS), 0.1),
                                 jnp.linspace(3.0, 6.0, ML_HEADS, dtype=f32) + nrm((nm, 2, 1, ML_HEADS), 0.1)], axis=2)
    return {
        "x": x,
        "ssd_norm": gain((na, D_MODEL)),
        "ssd_w_in": nrm((na, D_MODEL, SSD_PROJ), w_in_s),
        "ssd_conv_w": nrm((na, SSD_CONV, SSD_CONV_DIM), SSD_CONV ** -0.5),
        "ssd_conv_b": nrm((na, SSD_CONV_DIM), 0.02),
        "ssd_dt_bias": ssd_dt_bias,
        "ssd_a_log": ssd_a_log,
        "ssd_d": gain((na, SSD_HEADS)),
        "ssd_gnorm": gain((na, D_INNER)),
        "ssd_w_out": nrm((na, D_INNER, D_MODEL), w_out_s),
        "gla_norm": gain((nb, D_MODEL)),
        "gla_w_in": nrm((nb, D_MODEL, GLA_PROJ), w_in_s),
        "gla_w_gate": nrm((nb, 2, GLA_RANK, GLA_QK), GLA_RANK ** -0.5),
        "gla_b_gate": nrm((nb, 2, GLA_QK), 0.02),
        "gla_onorm": gain((nb, GLA_DV)),
        "gla_w_out": nrm((nb, D_INNER, D_MODEL), w_out_s),
        "hy_norm": gain((nh, D_MODEL)),
        "hy_w_in": nrm((nh, D_MODEL, HY_PROJ), w_in_s),
        "hy_conv_w": nrm((nh, HY_SHORT, 3 * D_INNER), HY_SHORT ** -0.5),
        "hy_conv_b": nrm((nh, 3 * D_INNER), 0.02),
        "hy_ffn_w_in": nrm((nh, HY_EMB, HY_FFN), HY_EMB ** -0.5),
        "hy_ffn_b_in": nrm((nh, HY_FFN), 0.1),
        "hy_ffn_w_hid": nrm((nh, HY_INNER, HY_FFN, HY_FFN), HY_FFN ** -0.5),
        "hy_ffn_b_hid": nrm((nh, HY_INNER, HY_FFN), 0.1),
        "hy_ffn_freq": gain((nh, HY_INNER + 1, HY_FFN)),
        "hy_ffn_w_out": nrm((nh, HY_FFN, HY_FILT), 0.05 * HY_FFN ** -0.5),
        "hy_d": nrm((nh, HY_ORDER, D_INNER), 1.0),
        "hy_w_out": nrm((nh, D_INNER, D_MODEL), w_out_s),
        "ml_norm": gain((nm, D_MODEL)),
        "ml_w_in": nrm((nm, D_MODEL, ML_PROJ), w_in_s),
        "ml_conv_w": nrm((nm, ML_CONV, D_INNER), ML_CONV ** -0.5),
        "ml_conv_b": nrm((nm, D_INNER), 0.02),
        "ml_w_q": nrm((nm, ML_HEADS, ML_DH, ML_DK), ML_DH ** -0.5),
        "ml_w_k": nrm((nm, ML_HEADS, ML_DH, ML_DK), ML_DH ** -0.5),
        "ml_w_v": nrm((nm, ML_HEADS, ML_DH, ML_DH), ML_DH ** -0.5),
        "ml_gate_b": ml_gate_b,
        "ml_skip": gain((nm, ML_HEADS, ML_DH)),
        "ml_onorm": gain((nm, ML_DH)),
        "ml_w_out": nrm((nm, D_INNER, D_MODEL), w_out_s),
        "final_norm": gain((D_MODEL,)),
    }

def first_block(x,
              ssd_norm, ssd_w_in, ssd_conv_w, ssd_conv_b, ssd_dt_bias, ssd_a_log, ssd_d, ssd_gnorm, ssd_w_out,
              gla_norm, gla_w_in, gla_w_gate, gla_b_gate, gla_onorm, gla_w_out,
              hy_norm, hy_w_in, hy_conv_w, hy_conv_b, hy_ffn_w_in, hy_ffn_b_in, hy_ffn_w_hid, hy_ffn_b_hid,
              hy_ffn_freq, hy_ffn_w_out, hy_d, hy_w_out,
              ml_norm, ml_w_in, ml_conv_w, ml_conv_b, ml_w_q, ml_w_k, ml_w_v, ml_gate_b, ml_skip, ml_onorm, ml_w_out,
              final_norm):
    h = x
    for i in range(DEPTH):
        kind, j = i % N_MIXERS, i // N_MIXERS
        if kind == 0:
            h = h + ssd_mixer(rmsnorm(h, ssd_norm[j]), ssd_w_in[j], ssd_conv_w[j], ssd_conv_b[j], ssd_dt_bias[j],
                              ssd_a_log[j], ssd_d[j], ssd_gnorm[j], ssd_w_out[j])
        elif kind == 1:
            h = h + gla_mixer(rmsnorm(h, gla_norm[j]), gla_w_in[j], gla_w_gate[j], gla_b_gate[j], gla_onorm[j],
                              gla_w_out[j])
        elif kind == 2:
            h = h + hyena_mixer(rmsnorm(h, hy_norm[j]), hy_w_in[j], hy_conv_w[j], hy_conv_b[j], hy_ffn_w_in[j],
                                hy_ffn_b_in[j], hy_ffn_w_hid[j], hy_ffn_b_hid[j], hy_ffn_freq[j], hy_ffn_w_out[j],
                                hy_d[j], hy_w_out[j])
        else:
            h = h + mlstm_mixer(rmsnorm(h, ml_norm[j]), ml_w_in[j], ml_conv_w[j], ml_conv_b[j], ml_w_q[j], ml_w_k[j],
                                ml_w_v[j], ml_gate_b[j], ml_skip[j], ml_onorm[j], ml_w_out[j])
    return rmsnorm(h, final_norm)


DEPTH_2 = 1

CONV_CH = D_MODEL // 2
CONV_WIDTH = 31
MLA_HEADS = 8
QK_NOPE = D_MODEL // 16
QK_ROPE = D_MODEL // 32
V_DIM = D_MODEL // 16
Q_LORA = 3 * D_MODEL // 8
KV_LORA = D_MODEL // 4
N_BRANCH = 2
IN_COLS = 2 * CONV_CH + Q_LORA + KV_LORA + QK_ROPE + N_BRANCH * D_MODEL
MEM_LEN = 256
X_HEADS = 4
X_HEAD_DIM = D_MODEL // 8
D_FF = 4 * D_MODEL
Q_BLOCK = 128
ROPE_THETA = 10000.0


def rms_norm(x, g):
    xf = x.astype(jnp.float32)
    y = xf * lax.rsqrt(jnp.mean(xf * xf, axis=-1, keepdims=True) + EPS)
    return (y * g.astype(jnp.float32)).astype(x.dtype)

def layer_norm(x, g, b):
    xf = x.astype(jnp.float32)
    mu = jnp.mean(xf, axis=-1, keepdims=True)
    var = jnp.mean(jnp.square(xf - mu), axis=-1, keepdims=True)
    y = (xf - mu) * lax.rsqrt(var + EPS)
    return (y * g.astype(jnp.float32) + b.astype(jnp.float32)).astype(x.dtype)

def rope_tables(positions):
    half = QK_ROPE // 2
    inv_freq = ROPE_THETA ** (-jnp.arange(half, dtype=jnp.float32) / half)
    ang = positions.astype(jnp.float32)[..., None] * inv_freq
    return jnp.cos(ang), jnp.sin(ang)

def apply_rope(t, cos, sin):
    half = t.shape[-1] // 2
    t1, t2 = t[..., :half], t[..., half:]
    c, s = cos.astype(t.dtype), sin.astype(t.dtype)
    return jnp.concatenate([t1 * c - t2 * s, t2 * c + t1 * s], axis=-1)

def conformer_conv(conv_in, conv_w, conv_b, ln_g, ln_b, w_conv_out):
    a, gt = jnp.split(conv_in, 2, axis=-1)
    z = a * jax.nn.sigmoid(gt)
    rhs = conv_w.astype(z.dtype).reshape(CONV_WIDTH, 1, CONV_CH)
    z = lax.conv_general_dilated(
        z, rhs, window_strides=(1,), padding=[(CONV_WIDTH - 1, 0)],
        dimension_numbers=("NWC", "WIO", "NWC"), feature_group_count=CONV_CH)
    z = z + conv_b
    z = layer_norm(z, ln_g, ln_b)
    z = jax.nn.silu(z)
    return z @ w_conv_out

def mla_attention(c_q, c_kv, k_rope_raw, cos, sin, q_norm_g, w_uq, kv_norm_g, w_ukv, w_mla_out):
    B, S, _ = c_q.shape
    q = rms_norm(c_q, q_norm_g) @ w_uq
    q = q.reshape(B, S, MLA_HEADS, QK_NOPE + QK_ROPE)
    q_nope, q_rope = q[..., :QK_NOPE], q[..., QK_NOPE:]
    q_rope = apply_rope(q_rope, cos[:, :, None, :], sin[:, :, None, :])
    kv = rms_norm(c_kv, kv_norm_g) @ w_ukv
    kv = kv.reshape(B, S, MLA_HEADS, QK_NOPE + V_DIM)
    k_nope, v = kv[..., :QK_NOPE], kv[..., QK_NOPE:]
    k_rope = apply_rope(k_rope_raw, cos, sin)

    scale = (QK_NOPE + QK_ROPE) ** -0.5
    n_blk = S // Q_BLOCK
    qn = (q_nope * scale).reshape(B, n_blk, Q_BLOCK, MLA_HEADS, QK_NOPE).transpose(1, 0, 2, 3, 4)
    qr = (q_rope * scale).reshape(B, n_blk, Q_BLOCK, MLA_HEADS, QK_ROPE).transpose(1, 0, 2, 3, 4)
    key_idx = jnp.arange(S)
    neg = jnp.finfo(jnp.float32).min

    def attend(args):
        qn_b, qr_b, blk = args
        s = jnp.einsum("bqhd,bkhd->bhqk", qn_b, k_nope, preferred_element_type=jnp.float32)
        s = s + jnp.einsum("bqhr,bkr->bhqk", qr_b, k_rope, preferred_element_type=jnp.float32)
        q_idx = blk * Q_BLOCK + jnp.arange(Q_BLOCK)
        mask = key_idx[None, :] <= q_idx[:, None]
        s = jnp.where(mask[None, None], s, neg)
        p = jax.nn.softmax(s, axis=-1).astype(v.dtype)
        return jnp.einsum("bhqk,bkhd->bqhd", p, v)

    o = lax.map(attend, (qn, qr, jnp.arange(n_blk)))
    o = o.transpose(1, 0, 2, 3, 4).reshape(B, S, MLA_HEADS * V_DIM)
    return o @ w_mla_out

def memory_cross_attention(u, mem_n, w_xq, w_xkv, w_xo):
    B, S, _ = u.shape
    q = (u @ w_xq).reshape(B, S, X_HEADS, X_HEAD_DIM) * (X_HEAD_DIM ** -0.5)
    kv = (mem_n @ w_xkv).reshape(B, MEM_LEN, 2, X_HEADS, X_HEAD_DIM)
    k, v = kv[:, :, 0], kv[:, :, 1]
    s = jnp.einsum("bqhd,bkhd->bhqk", q, k, preferred_element_type=jnp.float32)
    p = jax.nn.softmax(s, axis=-1).astype(v.dtype)
    o = jnp.einsum("bhqk,bkhd->bqhd", p, v).reshape(B, S, X_HEADS * X_HEAD_DIM)
    return o @ w_xo

def second_inputs(seed: int = 0) -> dict:
    key = jax.random.key(seed)
    ks = jax.random.split(key, 32)
    f32 = jnp.float32

    def w(k, shape, fan_in):
        return jax.random.normal(k, shape, f32) * (fan_in ** -0.5)

    def gain(k, shape):
        return 1.0 + 0.02 * jax.random.normal(k, shape, f32)

    L = DEPTH_2
    x = jax.random.normal(ks[0], (BATCH, SEQ, D_MODEL), f32)
    mem = jax.random.normal(ks[1], (BATCH, MEM_LEN, D_MODEL), f32)
    offsets = jax.random.randint(ks[2], (BATCH, 1), 0, 4096, dtype=jnp.int32)
    positions = offsets + jnp.arange(SEQ, dtype=jnp.int32)[None, :]
    return {
        "x": x,
        "mem": mem,
        "positions": positions,
        "norm_mix_g": gain(ks[3], (L, D_MODEL)),
        "w_in": w(ks[4], (L, D_MODEL, IN_COLS), D_MODEL),
        "conv_w": w(ks[5], (L, CONV_WIDTH, CONV_CH), CONV_WIDTH),
        "conv_b": 0.02 * jax.random.normal(ks[6], (L, CONV_CH), f32),
        "conv_ln_g": gain(ks[7], (L, CONV_CH)),
        "conv_ln_b": 0.02 * jax.random.normal(ks[8], (L, CONV_CH), f32),
        "w_conv_out": w(ks[9], (L, CONV_CH, D_MODEL), CONV_CH),
        "q_norm_g": gain(ks[10], (L, Q_LORA)),
        "w_uq": w(ks[11], (L, Q_LORA, MLA_HEADS * (QK_NOPE + QK_ROPE)), Q_LORA),
        "kv_norm_g": gain(ks[12], (L, KV_LORA)),
        "w_ukv": w(ks[13], (L, KV_LORA, MLA_HEADS * (QK_NOPE + V_DIM)), KV_LORA),
        "w_mla_out": w(ks[14], (L, MLA_HEADS * V_DIM, D_MODEL), MLA_HEADS * V_DIM),
        "w_out": w(ks[15], (L, D_MODEL, D_MODEL), D_MODEL),
        "norm_xattn_g": gain(ks[16], (L, D_MODEL)),
        "norm_mem_g": gain(ks[17], (L, D_MODEL)),
        "w_xq": w(ks[18], (L, D_MODEL, X_HEADS * X_HEAD_DIM), D_MODEL),
        "w_xkv": w(ks[19], (L, D_MODEL, 2 * X_HEADS * X_HEAD_DIM), D_MODEL),
        "w_xo": w(ks[20], (L, X_HEADS * X_HEAD_DIM, D_MODEL), X_HEADS * X_HEAD_DIM),
        "norm_mlp_g": gain(ks[21], (L, D_MODEL)),
        "w_mlp1": w(ks[22], (L, D_MODEL, D_FF), D_MODEL),
        "w_mlp2": w(ks[23], (L, D_FF, D_MODEL), D_FF),
        "final_norm_g": gain(ks[24], (D_MODEL,)),
    }

def second_block(x, mem, positions, norm_mix_g, w_in, conv_w, conv_b, conv_ln_g, conv_ln_b,
              w_conv_out, q_norm_g, w_uq, kv_norm_g, w_ukv, w_mla_out, w_out,
              norm_xattn_g, norm_mem_g, w_xq, w_xkv, w_xo, norm_mlp_g, w_mlp1, w_mlp2,
              final_norm_g):
    cos, sin = rope_tables(positions)
    B, S, _ = x.shape
    cut = np.cumsum([2 * CONV_CH, Q_LORA, KV_LORA, QK_ROPE]).tolist()
    h = x
    for l in range(DEPTH_2):
        u = rms_norm(h, norm_mix_g[l])
        proj = u @ w_in[l]
        conv_in, c_q, c_kv, k_rope_raw, gate_logits = jnp.split(proj, cut, axis=-1)
        conv_out = conformer_conv(conv_in, conv_w[l], conv_b[l], conv_ln_g[l], conv_ln_b[l],
                                  w_conv_out[l])
        mla_out = mla_attention(c_q, c_kv, k_rope_raw, cos, sin, q_norm_g[l], w_uq[l],
                                kv_norm_g[l], w_ukv[l], w_mla_out[l])
        gates = jax.nn.sigmoid(gate_logits).reshape(B, S, N_BRANCH, D_MODEL)
        merged = gates[:, :, 0] * conv_out + gates[:, :, 1] * mla_out
        h = h + merged @ w_out[l]
        u = rms_norm(h, norm_xattn_g[l])
        mem_n = rms_norm(mem, norm_mem_g[l])
        h = h + memory_cross_attention(u, mem_n, w_xq[l], w_xkv[l], w_xo[l])
        u = rms_norm(h, norm_mlp_g[l])
        h = h + jnp.square(jax.nn.relu(u @ w_mlp1[l])) @ w_mlp2[l]
    return rms_norm(h, final_norm_g)


def setup_inputs(seed=0):
    out = dict(first_inputs(seed))
    for name, value in second_inputs(seed + 1).items():
        if name != "x":
            out[name + "_2"] = value
    return out


def reference(
    x, ssd_norm, ssd_w_in, ssd_conv_w, ssd_conv_b, ssd_dt_bias, ssd_a_log, ssd_d, ssd_gnorm,
    ssd_w_out, gla_norm, gla_w_in, gla_w_gate, gla_b_gate, gla_onorm, gla_w_out, hy_norm,
    hy_w_in, hy_conv_w, hy_conv_b, hy_ffn_w_in, hy_ffn_b_in, hy_ffn_w_hid, hy_ffn_b_hid,
    hy_ffn_freq, hy_ffn_w_out, hy_d, hy_w_out, ml_norm, ml_w_in, ml_conv_w, ml_conv_b, ml_w_q,
    ml_w_k, ml_w_v, ml_gate_b, ml_skip, ml_onorm, ml_w_out, final_norm, mem_2, positions_2,
    norm_mix_g_2, w_in_2, conv_w_2, conv_b_2, conv_ln_g_2, conv_ln_b_2, w_conv_out_2,
    q_norm_g_2, w_uq_2, kv_norm_g_2, w_ukv_2, w_mla_out_2, w_out_2, norm_xattn_g_2,
    norm_mem_g_2, w_xq_2, w_xkv_2, w_xo_2, norm_mlp_g_2, w_mlp1_2, w_mlp2_2, final_norm_g_2,
):
    x = first_block(
        x, ssd_norm, ssd_w_in, ssd_conv_w, ssd_conv_b, ssd_dt_bias, ssd_a_log, ssd_d, ssd_gnorm,
        ssd_w_out, gla_norm, gla_w_in, gla_w_gate, gla_b_gate, gla_onorm, gla_w_out, hy_norm,
        hy_w_in, hy_conv_w, hy_conv_b, hy_ffn_w_in, hy_ffn_b_in, hy_ffn_w_hid, hy_ffn_b_hid,
        hy_ffn_freq, hy_ffn_w_out, hy_d, hy_w_out, ml_norm, ml_w_in, ml_conv_w, ml_conv_b,
        ml_w_q, ml_w_k, ml_w_v, ml_gate_b, ml_skip, ml_onorm, ml_w_out, final_norm,
    )
    return second_block(
        x, mem_2, positions_2, norm_mix_g_2, w_in_2, conv_w_2, conv_b_2, conv_ln_g_2,
        conv_ln_b_2, w_conv_out_2, q_norm_g_2, w_uq_2, kv_norm_g_2, w_ukv_2, w_mla_out_2,
        w_out_2, norm_xattn_g_2, norm_mem_g_2, w_xq_2, w_xkv_2, w_xo_2, norm_mlp_g_2, w_mlp1_2,
        w_mlp2_2, final_norm_g_2,
    )


_drawn_inputs = setup_inputs


def setup_inputs(seed=0):
    import zlib

    import numpy as np

    out = dict(_drawn_inputs(seed))
    spreads = {}
    factors = {'ssd_d': 5.594,
     'ssd_gnorm': 3.005,
     'gla_norm': 3.199,
     'gla_b_gate': 8.0,
     'gla_onorm': 6.421,
     'norm_mix_g_2': 6.617,
     'conv_b_2': 4.364,
     'conv_ln_g_2': 7.59,
     'conv_ln_b_2': 8.0,
     'q_norm_g_2': 8.0,
     'kv_norm_g_2': 8.0,
     'norm_xattn_g_2': 8.0,
     'norm_mem_g_2': 8.0,
     'norm_mlp_g_2': 10.12,
     'final_norm_g_2': 7.969}
    for name, (base, spread) in spreads.items():
        noise = np.random.default_rng([zlib.crc32(name.encode()), seed]).standard_normal(out[name].shape)
        drawn = base * np.exp(spread * noise) if base else spread * noise
        out[name] = jnp.asarray(drawn.astype(out[name].dtype))
    for name, factor in factors.items():
        out[name] = (out[name] * factor).astype(out[name].dtype)
    return out
```

```python
from concourse import mybir
from contextlib import ExitStack

F32 = mybir.dt.float32
F32R = mybir.dt.float32r
I32 = mybir.dt.int32
ACT = mybir.ActivationFunctionType
ALU = mybir.AluOpType
AX = mybir.AxisListType

P = 128
T = 512
NT = T // P
D = 1024
KT = D // P
EPS = 1e-6
LN_EXP = "natural_log_exp_and_others"
SI = 2048
SG = 8
SH = 32
HPG = SH // SG
HD = 64
GW = SI // SG
GH = 4
GV = 512
UNIT = 1024
RAW = 2
WS = 3
SB = 3


class Ctx:
    pass


def stage_semaphores(nc, ctx, tag):
    used = []

    def sem(name):
        used.append(nc.alloc_semaphore(name=tag + name))
        return used[-1]

    def clear():
        nc.clear_and_free_semaphores(used)
        nc.all_engine_barrier()

    ctx.callback(clear)
    return sem


def mm3(pe, out, lh, ll, rh, rl, first, last, skip=False):
    pe.matmul(out, lh, rl, start=first, stop=False, skip_group_check=skip)
    pe.matmul(out, ll, rh, start=False, stop=False, skip_group_check=skip)
    return pe.matmul(out, lh, rh, start=False, stop=last, skip_group_check=skip)


def spread(ap, n):
    return ap.rearrange("p (a o) -> p a o", o=1).broadcast_to([ap.shape[0], ap.shape[1], n])


def again(ap, n):
    return ap.rearrange("p (o a) -> p o a", o=1).broadcast_to([ap.shape[0], n, ap.shape[1]])


def add_units(c, views, tiles, m=P):
    first = len(c.units)
    for v in views:
        parts = v if isinstance(v, list) else [(0, v)]
        slot = len(c.units) % RAW
        c.arrived[slot] += 16 * len(parts)
        c.units.append((parts[0][1].shape[1], max(a + v.shape[2] for a, v in parts), parts, c.arrived[slot], m))
        c.tiles_before.append(c.tiles_before[-1] + tiles)
    return first


def raw_view(c, n):
    kt, cols = c.units[n][:2]
    return c.raw[:, n % RAW, 0:kt * cols].rearrange("p (k m) -> p k m", k=kt)


def w_view(c, n):
    kt, cols = c.units[n][:2]
    cut = [w[:, n % WS, 0:kt * cols].rearrange("p (k m) -> p k m", k=kt) for w in (c.w_hi, c.w_lo)]
    return cut[0], cut[1]


def load_unit(c, sp, n):
    if n >= len(c.units) or n < c.loaded:
        return
    c.loaded = n + 1
    if n >= RAW:
        sp.wait_ge(c.w_split, n - RAW + 1)
    for a, view in c.units[n][2]:
        sp.dma_start(raw_view(c, n)[:, :, a:a + view.shape[2]], view).then_inc(c.w_loaded[n % RAW], 16)


def split_hi(c, act, n):
    if n >= len(c.units) or n < c.hi_next:
        return
    c.hi_next = n + 1
    act.wait_ge(c.w_loaded[n % RAW], c.units[n][3])
    if n >= WS:
        act.wait_ge(c.tile_done, c.tiles_before[n - WS + 1])
    act.activation(w_view(c, n)[0], raw_view(c, n), ACT.Copy).then_inc(c.w_rounded, 1)


def split_lo(c, dve, n):
    if n >= len(c.units) or n < c.lo_next:
        return
    c.lo_next = n + 1
    dve.wait_ge(c.w_rounded, n + 1)
    hi, lo = w_view(c, n)
    dve.tensor_tensor(lo, raw_view(c, n), hi.bitcast(F32), ALU.subtract).then_inc(c.w_split, 1)


def bank(c, t):
    return c.stream[t % SB]


def free_value(c, t):
    return c.bank_free[t % SB], t // SB + 1


def stream_products(c, pe, n, xh, xl, width=T, ready=None):
    if n < c.streamed:
        return
    c.streamed = n + 1
    kt, cols, _, _, rows = c.units[n]
    hi, lo = w_view(c, n)
    pe.wait_ge(c.w_split, n + 1)
    for j in range(cols // rows):
        t = c.tiles_before[n] + j
        if t >= SB:
            pe.wait_ge(c.bank_free[t % SB], t // SB)
        m = slice(j * rows, (j + 1) * rows)
        for k in range(kt):
            if ready and j == 0:
                pe.wait_ge(*ready(k))
            last = mm3(pe, bank(c, t)[0:rows, 0:width], hi[:, k, m], lo[:, k, m], xh(k), xl(k), k == 0,
                       k == kt - 1)
        last.then_inc(c.tile_done, 1)


def refine_rstd(dve, done, n, r, tmp, sums, width):
    dve.tensor_scalar(tmp, sums, -0.5 / width, -0.5 * EPS, ALU.mult, ALU.add).then_inc(done, 1)
    dve.wait_ge(done, n + 1)
    dve.tensor_tensor(tmp, tmp, r, ALU.mult).then_inc(done, 1)
    dve.wait_ge(done, n + 2)
    dve.tensor_tensor(tmp, tmp, r, ALU.mult).then_inc(done, 1)
    dve.wait_ge(done, n + 3)
    dve.scalar_tensor_tensor(out=r, in0=tmp, scalar=1.5, in1=r, op0=ALU.add, op1=ALU.mult).then_inc(done, 1)
    dve.wait_ge(done, n + 4)


def start_stage(nc, c, A):
    with ExitStack() as ctx:
        sb = lambda n, s, d=F32: ctx.enter_context(nc.sbuf_tensor(n, s, d))
        sem = stage_semaphores(nc, ctx, "")
        xrow = sb("x_rows", [P, NT, D])
        prow = sb("param_rows", [P, len(c.ptiles), P])
        s_zero, s_const, s_x = sem("zeroed"), sem("constants"), sem("x_loaded")
        s_prow, s_tp, s_ev = sem("params_loaded"), sem("transposed"), sem("evacuated")
        s_dl = sem("skips_loaded")
        skips = sb("skips", [P, SH])
        nq = sum(len(t) for t in c.ptiles)
        with nc.Block() as block:
            @block.sync
            def _(sp):
                sp.dma_start(xrow[:, :, :], A["x"][0].rearrange("(t p) d -> p t d", p=P)).then_inc(s_x, 16)
                for i, tile in enumerate(c.ptiles):
                    for r0, view in tile:
                        dst = prow[r0:r0 + view.shape[0], i, :]
                        if len(view.shape) == 3:
                            dst = dst.rearrange("p (a b) -> p a b", a=view.shape[1])
                        sp.dma_start(dst, view).then_inc(s_prow, 16)
                sp.dma_start(skips[:, :], A["ssd_d"][0:1, :].broadcast_to([P, SH])).then_inc(s_dl, 16)

            @block.gpsimd
            def _(pool):
                pool.memset(c.ones[:, :], 1.0).then_inc(s_zero, 1)
                pool.memset(c.ident[:, :], 0.0).then_inc(s_zero, 1)
                pool.wait_ge(s_zero, 2)
                sel = pool.affine_select
                sel(out=c.ident[:, :], in_=c.ident[:, :], compare_op=ALU.not_equal, fill=1.0, base=0,
                    pattern=[[-1, P]], channel_multiplier=1).then_inc(s_const, 1)
                sel(out=c.ident_r[:, :], in_=c.ones[:, :], compare_op=ALU.is_equal, fill=0.0, base=0,
                    pattern=[[-1, P]], channel_multiplier=1).then_inc(s_const, 1)
                sel(out=c.ge[:, :], in_=c.ones[:, :], compare_op=ALU.is_ge, fill=0.0, base=0,
                    pattern=[[1, P]], channel_multiplier=-1).then_inc(s_const, 1)
                sel(out=c.le[:, :], in_=c.ones[:, :], compare_op=ALU.is_ge, fill=0.0, base=0,
                    pattern=[[-1, P]], channel_multiplier=1).then_inc(s_const, 1)
                sel(out=c.gt_r[:, :], in_=c.ones[:, :], compare_op=ALU.is_gt, fill=0.0, base=0,
                    pattern=[[-1, P]], channel_multiplier=1).then_inc(s_const, 1)
                sel(out=c.lt_r[:, :], in_=c.ones[:, :], compare_op=ALU.is_gt, fill=0.0, base=0,
                    pattern=[[1, P]], channel_multiplier=-1).then_inc(s_const, 1)
                pool.memset(c.eps[:, :], EPS).then_inc(s_const, 1)

            @block.tensor
            def _(pe):
                pe.wait_ge(s_const, 1)
                pe.wait_ge(s_x, 16)
                for k in range(KT):
                    if k >= 4:
                        pe.wait_ge(s_ev, k - 3)
                    for t in range(NT):
                        last = pe.transpose(c.q[k % 4][:, t * P:(t + 1) * P], xrow[:, t, k * P:(k + 1) * P],
                                            c.ident[:, :])
                    last.then_inc(s_tp, 1)
                pe.wait_ge(s_prow, 16 * nq)
                for i in range(len(c.ptiles)):
                    pe.wait_ge(s_ev, KT + i - 3)
                    n = c.prows[i]
                    pe.transpose(c.q[(KT + i) % 4][:, 0:n], prow[0:n, i, :], c.ident[0:n, 0:n]).then_inc(s_tp, 1)

            @block.vector
            def _(dve):
                for k in range(KT):
                    dve.wait_ge(s_tp, k + 1)
                    dve.tensor_copy(c.h[:, k, :], c.q[k % 4][:, :]).then_inc(s_ev, 1)
                for i in range(len(c.ptiles)):
                    dve.wait_ge(s_tp, KT + i + 1)
                    n = c.prows[i]
                    dve.tensor_copy(c.par[:, i * P:i * P + n], c.q[(KT + i) % 4][:, 0:n]).then_inc(s_ev, 1)
                dve.wait_ge(s_dl, 16)
                a = c.at["ssd_d"]
                for e in range(2):
                    dve.tensor_copy(c.par[e * HD:(e + 1) * HD, a:a + SH // 2],
                                    skips[e * HD:(e + 1) * HD, e:SH:2]).then_inc(s_ev, 1)


def square_tile(c, act, m, final):
    n = c.squared
    c.squared += 1
    act.wait_ge(*final)
    if n >= 2:
        act.wait_ge(c.square_added, n - 1)
    act.activation(c.sq[:, n % 2, :], c.h[:, m, :], ACT.Square).then_inc(c.square_ready, 1)


def add_squares(c, pool):
    for m in range(KT):
        n = c.added
        c.added += 1
        pool.wait_ge(c.square_ready, n + 1)
        if m == 0:
            pool.tensor_copy(c.sumsq[:, :], c.sq[:, n % 2, :]).then_inc(c.square_added, 1)
        else:
            pool.wait_ge(c.square_added, n)
            pool.tensor_tensor(c.sumsq[:, :], c.sumsq[:, :], c.sq[:, n % 2, :], ALU.add).then_inc(c.square_added, 1)


def norm_stage(nc, c, tag, src, kt, g, uh, ul, plain=None, summed=False, sum_next=False):
    width = kt * P
    with ExitStack() as ctx:
        sb = lambda n, s, d=F32: ctx.enter_context(nc.sbuf_tensor(tag + n, s, d))
        sem = stage_semaphores(nc, ctx, tag)
        NB = 4
        buf = sb("_squares", [P, NB, T])
        acc = c.sumsq if summed else sb("_sum", [P, T])
        rstd = sb("_rstd", [P, T])
        tmp = sb("_newton", [P, T])
        s_sq, s_acc, s_sum, s_half, s_rs, s_fine, s_un, s_uh, s_ul, s_up = (sem(n) for n in (
            "_squared", "_accumulated", "_summed", "_halved", "_rstd_s", "_refined", "_normed_s", "_rounded",
            "_rest_even", "_rest_odd"))
        n0 = c.next_unit
        split = plain is None
        with nc.Block() as block:
            @block.sync
            def _(sp):
                for n in range(n0, n0 + RAW):
                    load_unit(c, sp, n)

            @block.scalar
            def _(act):
                act.preload_act_table_set(LN_EXP)
                for k in range(0 if summed else kt):
                    if k >= NB:
                        act.wait_ge(s_acc, k - NB if k > NB else 1)
                    act.activation(buf[:, k % NB, :], src(k), ACT.Square).then_inc(s_sq, 1)
                for n in range(n0, n0 + 2):
                    split_hi(c, act, n)
                act.wait_ge(s_half, 1)
                act.activation(rstd[:, :], tmp[:, :], ACT.Ln, scale=-2.0).then_inc(s_rs, 1)
                act.wait_ge(s_rs, 1)
                act.activation(rstd[:, :], rstd[:, :], ACT.Exp, scale=-0.5).then_inc(s_rs, 1)
                if split:
                    for k in range(kt):
                        act.wait_ge(s_un, k + 1)
                        act.activation(uh(k), buf[:, k % NB, :], ACT.Copy).then_inc(s_uh, 1)
                if sum_next:
                    for k in range(kt):
                        square_tile(c, act, k, (s_un, k + 1))

            @block.tensor
            def _(pe):
                pe.wait_ge(*((c.square_added, c.added) if summed else (s_acc, kt - 1)))
                pe.matmul(c.q[0][:, :], c.ones[:, :], acc[:, :], start=True, stop=True).then_inc(s_sum, 1)
                if split:
                    stream_products(c, pe, n0, uh, ul,
                                    ready=lambda k: (s_ul, k // 2 + 1) if k % 2 == 0 else (s_up, k // 2 + 1))

            @block.gpsimd
            def _(pool):
                if sum_next:
                    add_squares(c, pool)
                if split:
                    for k in range(1, kt, 2):
                        pool.wait_ge(s_uh, k + 1)
                        pool.tensor_tensor(ul(k), buf[:, k % NB, :], uh(k).bitcast(F32), ALU.subtract)\
                            .then_inc(s_up, 1)

            @block.vector
            def _(dve):
                for k in range(1, 1 if summed else kt):
                    dve.wait_ge(s_sq, k + 1)
                    if k > 1:
                        dve.wait_ge(s_acc, k - 1)
                    dve.tensor_tensor(acc[:, :], buf[:, 0, :] if k == 1 else acc[:, :], buf[:, k % NB, :], ALU.add)\
                       .then_inc(s_acc, 1)
                for n in range(n0, n0 + 2):
                    split_lo(c, dve, n)
                dve.wait_ge(s_sum, 1)
                dve.tensor_scalar(tmp[:, :], c.q[0][:, :], -0.5 / width, -0.5 * EPS, ALU.mult, ALU.add)\
                   .then_inc(s_half, 1)
                dve.wait_ge(s_half, 1)
                dve.wait_ge(s_rs, 2)
                dve.tensor_tensor(tmp[:, :], tmp[:, :], rstd[:, :], ALU.mult).then_inc(s_fine, 1)
                dve.wait_ge(s_fine, 1)
                dve.tensor_tensor(tmp[:, :], tmp[:, :], rstd[:, :], ALU.mult).then_inc(s_fine, 1)
                dve.wait_ge(s_fine, 2)
                dve.scalar_tensor_tensor(out=rstd[:, :], in0=tmp[:, :], scalar=1.5, in1=rstd[:, :], op0=ALU.add,
                                         op1=ALU.mult).then_inc(s_fine, 1)
                dve.wait_ge(s_fine, 3)
                for k in range(kt + 2):
                    if k < kt:
                        if split and k >= NB:
                            dve.wait_ge(*((s_ul, (k - NB) // 2 + 1) if k % 2 == 0 else (s_up, (k - NB) // 2 + 1)))
                        dst = buf[:, k % NB, :] if split else plain(k)
                        dve.scalar_tensor_tensor(out=dst, in0=src(k), scalar=g(k), in1=rstd[:, :],
                                                 op0=ALU.mult, op1=ALU.mult).then_inc(s_un, 1)
                    if split and k >= 2 and k % 2 == 0:
                        e = k - 2
                        dve.wait_ge(s_uh, e + 1)
                        dve.tensor_tensor(ul(e), buf[:, e % NB, :], uh(e).bitcast(F32), ALU.subtract)\
                           .then_inc(s_ul, 1)


SSD_SLOTS = 8
SSD_ROUNDS = SG + 2


def ssd_units(c, A):
    w_in, w_out = A["ssd_w_in"][0], A["ssd_w_out"][0]
    kview = lambda c0: w_in[:, c0:c0 + P].rearrange("(k p) m -> p k m", p=P)
    X0, B0, C0 = SI, 2 * SI, 2 * SI + SG * P
    NU, NI = SSD_SLOTS, SSD_ROUNDS
    plan, n = {}, len(c.units)
    for i in range(NI):
        for k in range(NU):
            closes = k in (4, 7)
            g = i - 2 if closes else i
            if not 0 <= g < SG:
                continue
            if closes:
                half = (k - 4) // 3
                v = w_out[g * GW:(g + 1) * GW, half * 512:half * 512 + 512].rearrange("(k p) m -> p k m", p=P)
                add_units(c, [v], 4)
            else:
                col = {0: g * GW, 1: g * GW + P, 2: X0 + g * GW, 3: X0 + g * GW + P, 5: B0 + g * P,
                       6: C0 + g * P}[k]
                add_units(c, [kview(col)], 1)
            plan[i, k] = n
            n += 1
    return plan


def ssd_stage(nc, c, A, plan):
    par, at = c.par, c.at
    w_in = A["ssd_w_in"][0]
    NU, NI = SSD_SLOTS, SSD_ROUNDS
    slots = [(i, k) for i in range(NI) for k in range(NU)] + [(NI, 0)]
    first = c.next_unit
    c.next_unit = first + len(plan)

    with ExitStack() as ctx:
        sb = lambda n, s, d=F32: ctx.enter_context(nc.sbuf_tensor("ssd_" + n, s, d))
        sem = stage_semaphores(nc, ctx, "ssd_")
        dtc = sb("dt_cols", [P, NT, 64])
        lah = sb("la_hi_cols", [P, NT, 64])
        lal = sb("la_lo_cols", [P, NT, 64])
        wc = sb("w_cols", [P, NT, 64])
        et = sb("total_cols", [P, NT, 64])
        cum_h = sb("cum_hi", [64, T], F32R)
        cum_l = sb("cum_lo", [64, T], F32R)

        with ExitStack() as pre:
            pb = lambda n, s, d=F32: pre.enter_context(nc.sbuf_tensor("dt_" + n, s, d))
            wdt = pb("w", [P, KT, 64])
            una = pb("u", [P, 2, T])
            raw = pb("raw", [64, T])
            e = pb("e", [64, T])
            s1 = pb("s1", [64, T])
            s2 = pb("s2", [64, T])
            ser = pb("series", [64, T])
            dt = pb("dt", [64, T])
            la = pb("la", [64, T])
            cum = pb("cum", [64, T])
            lac = pb("la_cols", [P, NT, 64])
            cumc = pb("cum_cols", [P, NT, 64])
            lahr = pb("la_round", [P, NT, 64], F32R)
            vec = pb("vec", [64, 4])
            go = pb("restart", [64, T])
            s_go = sem("dt_restart")
            s_w, s_u, s_mm, s_a, s_v, s_d1, s_t = (sem(n) for n in ("dt_w", "dt_u", "dt_mm", "dt_act", "dt_dve",
                                                                  "dt_soft", "dt_t"))
            with nc.Block() as block:
                @block.sync
                def _(sp):
                    sp.dma_start(wdt[:, :, :], w_in[:, 3 * SI:3 * SI + 64].rearrange("(k p) m -> p k m", p=P)).then_inc(s_w, 16)
                    sp.dma_start(vec[:, 0:1], A["ssd_dt_bias"][0].rearrange("a (h o) -> (a h) o", o=1))\
                      .then_inc(s_w, 16)
                    sp.dma_start(vec[:, 1:2], A["ssd_a_log"][0].rearrange("a (h o) -> (a h) o", o=1))\
                      .then_inc(s_w, 16)
                    for n in range(first, first + 4):
                        load_unit(c, sp, n)

                @block.gpsimd
                def _(pool):
                    pool.memset(go[:, :], 1.0).then_inc(s_go, 1)
                    pool.wait_ge(s_go, 1)
                    pool.memset(go[0:32, 0:T:P], 0.0).then_inc(s_go, 1)
                    pool.memset(go[32:64, P - 1:T:P], 0.0).then_inc(s_go, 1)

                @block.tensor
                def _(pe):
                    pe.wait_ge(s_w, 48)
                    for k in range(KT):
                        pe.wait_ge(s_u, k + 1)
                        pe.matmul(c.q[0][0:64, :], wdt[:, k, :], una[:, k % 2, :], start=k == 0,
                                  stop=k == KT - 1).then_inc(s_mm, 1)
                    for n in (first + 1, first + 2):
                        stream_products(c, pe, n, lambda j: c.uh[:, j, :], lambda j: c.ul[:, j, :])
                    pe.wait_ge(s_v, 14)
                    for j, src in enumerate((dt, la, cum)):
                        for t in range(NT):
                            last = pe.transpose(c.q[1 + j][:, t * 64:(t + 1) * 64], src[:, t * P:(t + 1) * P],
                                                c.ident[0:64, 0:64])
                    last.then_inc(s_t, 1)
                    pe.wait_ge(s_v, 16)
                    pe.matmul(c.q[0][:, 0:NT * 64], c.ones[:, :], lac[:, :, :].rearrange("p t h -> p (t h)"),
                              start=True, stop=True).then_inc(s_t, 1)

                @block.scalar
                def _(act):
                    act.wait_ge(s_w, 48)
                    act.activation(vec[:, 2:3], vec[:, 1:2], ACT.Exp).then_inc(s_a, 1)
                    for n in (first + 2, first + 3):
                        split_hi(c, act, n)
                    act.wait_ge(s_mm, KT)
                    act.activation(raw[:, :], c.q[0][0:64, :], ACT.Identity, bias=vec[:, 0:1]).then_inc(s_a, 1)
                    act.wait_ge(s_a, 2)
                    act.activation(e[:, :], raw[:, :], ACT.Abs).then_inc(s_a, 1)
                    act.wait_ge(s_a, 3)
                    act.activation(e[:, :], e[:, :], ACT.Exp, scale=-1.0).then_inc(s_a, 1)
                    act.wait_ge(s_v, 13)
                    act.activation(cum_h[:, :], cum[:, :], ACT.Copy).then_inc(s_a, 1)
                    act.wait_ge(s_v, 18)
                    act.activation(cumc[:, :, :], cumc[:, :, :], ACT.Exp).then_inc(s_a, 1)
                    act.activation(et[:, :, :].rearrange("p t h -> p (t h)"), c.q[0][:, 0:NT * 64], ACT.Exp)\
                       .then_inc(s_a, 1)
                    act.activation(lahr[:, :, :], lac[:, :, :], ACT.Copy).then_inc(s_a, 1)

                @block.vector
                def _(dve):
                    for k in range(KT):
                        if k >= 2:
                            dve.wait_ge(s_mm, k - 1)
                        dve.tensor_tensor(una[:, k % 2, :], c.uh[:, k, :].bitcast(F32),
                                          c.ul[:, k, :].bitcast(F32), ALU.add).then_inc(s_u, 1)
                    for n in (first + 2, first + 3):
                        split_lo(c, dve, n)
                    dve.wait_ge(s_a, 4)
                    dve.tensor_scalar(s1[:, :], e[:, :], 2.0, None, ALU.add).then_inc(s_v, 1)
                    dve.wait_ge(s_v, 1)
                    dve.reciprocal(s1[:, :], s1[:, :]).then_inc(s_v, 1)
                    dve.wait_ge(s_v, 2)
                    dve.tensor_tensor(s1[:, :], s1[:, :], e[:, :], ALU.mult).then_inc(s_v, 1)
                    dve.wait_ge(s_v, 3)
                    dve.tensor_tensor(s2[:, :], s1[:, :], s1[:, :], ALU.mult).then_inc(s_v, 1)
                    dve.wait_ge(s_v, 4)
                    dve.tensor_scalar(ser[:, :], s2[:, :], 1.0 / 15, None, ALU.mult).then_inc(s_v, 1)
                    for j, d in enumerate((13, 11, 9, 7, 5, 3)):
                        dve.wait_ge(s_v, 5 + j)
                        dve.scalar_tensor_tensor(out=ser[:, :], in0=ser[:, :], scalar=1.0 / d, in1=s2[:, :],
                                                 op0=ALU.add, op1=ALU.mult).then_inc(s_v, 1)
                    dve.wait_ge(s_v, 11)
                    dve.scalar_tensor_tensor(out=ser[:, :], in0=ser[:, :], scalar=1.0, in1=s1[:, :],
                                             op0=ALU.add, op1=ALU.mult).then_inc(s_d1, 1)
                    dve.tensor_scalar(raw[:, :], raw[:, :], 0.0, None, ALU.max).then_inc(s_d1, 1)
                    dve.wait_ge(s_d1, 2)
                    dve.scalar_tensor_tensor(out=dt[:, :], in0=ser[:, :], scalar=2.0, in1=raw[:, :],
                                             op0=ALU.mult, op1=ALU.add).then_inc(s_d1, 1)
                    dve.wait_ge(s_d1, 3)
                    dve.tensor_scalar(la[:, :], dt[:, :], vec[:, 2:3], -1.0, ALU.mult, ALU.mult).then_inc(s_d1, 1)
                    dve.wait_ge(s_d1, 4)
                    dve.wait_ge(s_go, 3)
                    dve.tensor_tensor_scan(cum[0:32, :], go[0:32, :], la[0:32, :], 0.0, ALU.mult, ALU.add)\
                       .then_inc(s_v, 1)
                    dve.tensor_tensor_scan(cum[32:64, ::-1], go[32:64, ::-1], la[32:64, ::-1], 0.0, ALU.mult,
                                           ALU.add).then_inc(s_v, 1)
                    dve.wait_ge(s_a, 5)
                    dve.wait_ge(s_v, 13)
                    dve.tensor_tensor(cum_l[:, :], cum[:, :], cum_h[:, :].bitcast(F32), ALU.subtract)\
                       .then_inc(s_v, 1)
                    dve.wait_ge(s_t, 1)
                    flat = lambda b: b[:, :, :].rearrange("p t h -> p (t h)")
                    dve.tensor_copy(flat(dtc), c.q[1][:, 0:NT * 64]).then_inc(s_v, 1)
                    dve.tensor_copy(flat(lac), c.q[2][:, 0:NT * 64]).then_inc(s_v, 1)
                    dve.tensor_copy(flat(cumc), c.q[3][:, 0:NT * 64]).then_inc(s_v, 1)
                    dve.wait_ge(s_t, 2)
                    dve.wait_ge(s_v, 17)
                    dve.tensor_tensor(flat(cumc), c.q[0][:, 0:NT * 64], flat(cumc), ALU.subtract).then_inc(s_v, 1)
                    dve.wait_ge(s_a, 8)
                    dve.tensor_tensor(flat(wc), flat(dtc), flat(cumc), ALU.mult).then_inc(s_v, 1)
                    dve.tensor_copy(flat(lah), flat(lahr).bitcast(F32)).then_inc(s_v, 1)
                    dve.wait_ge(s_v, 20)
                    dve.tensor_tensor(flat(lal), flat(lac), flat(lah), ALU.subtract).then_inc(s_v, 1)

        main = ctx.enter_context(ExitStack())
        mb = lambda n, s, d=F32: main.enter_context(nc.sbuf_tensor("ssd_" + n, s, d))
        xt = mb("x", [P, 2, 2, T])
        bct = mb("bc", [P, 2, T])
        bch, bcl = mb("bc_hi", [P, 2, T], F32R), mb("bc_lo", [P, 2, T], F32R)
        zs = mb("z", [P, 2, 2, T])
        xph = mb("x_pair_hi", [P, NT, 2, 192], F32R)
        xpl = mb("x_pair_lo", [P, NT, 2, 192], F32R)
        work = mb("work", [P, 3, T])
        decay, t1, t2 = (work[:, j, :] for j in range(3))
        xwf = work[:, :, :].rearrange("p a b -> p (a b)").rearrange("p (d j m) -> p d j m", d=2, j=3)
        xwh, xwl = mb("xw_hi", [P, 2, 3, GW], F32R), mb("xw_lo", [P, 2, 3, GW], F32R)
        bth, btl = mb("b_tok_hi", [P, T], F32R), mb("b_tok_lo", [P, T], F32R)
        cbm = mb("cb", [P, 2, T])
        rhs = mb("la_steps", [P, 4, HPG, P], F32R)
        mh, ml = mb("m_hi", [P, HPG, P], F32R), mb("m_lo", [P, HPG, P], F32R)
        st = mb("state", [P, 2, GW])
        sth, stl = mb("state_hi", [P, 3, 2 * GW], F32R), mb("state_lo", [P, 3, 2 * GW], F32R)
        ex = mb("exp_cum", [P, 2, T])
        y = mb("y", [P, 2, T])
        parts = mb("state_parts", [P, 2 * (T - P)])
        rstd = parts[:, 0:T]
        s_fin = sem("y_complete")
        pick = mb("head_pick", [64, 4, P], F32R)
        s_pick = sem("head_pick_ready")
        yh, yl = mb("y_hi", [P, 2, T], F32R), mb("y_lo", [P, 2, T], F32R)
        q = c.q
        (s_center, s_tap, s_silu, s_zsilu, s_bch, s_bcl, s_tx, s_cb, s_xph, s_xpl, s_xw, s_xwh, s_xwl, s_cbm, s_rhs,
         s_arg, s_decay, s_t2, s_m, s_mh, s_ml, s_y, s_con, s_st, s_sh, s_sl, s_int, s_e, s_ee, s_asm, s_sq, s_nrm,
         s_rs, s_yn, s_yh, s_yl, s_clear) = (sem(n) for n in (
             "centre_tap", "taps", "conv_done", "gate_done", "bc_rounded", "bc_rest", "transposed", "cb_products",
             "xpair_rounded", "xpair_rest", "xw", "xw_rounded", "xw_rest", "cb_masked", "la_steps_ready",
             "decay_sums", "decays", "backward_part", "m_parts", "m_rounded", "m_rest", "y_intra", "contributions",
             "states", "state_rounded", "state_rest", "y_inter", "cum_spread", "exp_cum_ready", "assembled",
             "squared", "square_sums", "rstd_ready", "normed", "y_rounded", "y_rest", "cleared"))
        G = range(SG)
        CONV = {2: 0, 3: 1, 5: 2, 6: 3}

        def conv_tile(g, j):
            return (2 * g, 2 * g + 1, 2 * SG + g, 3 * SG + g)[j]

        def tap(k, ct):
            col = at["ssd_conv_w"] + k * 32 + ct
            return par[:, col:col + 1]

        def conv_out(g, j):
            return xt[:, g % 2, j, :] if j < 2 else bct[:, j - 2, :]

        def head(cols, d, t, g):
            return cols[:, t, 32 * d + HPG * g:32 * d + HPG * (g + 1)]

        def unit_in(i, k):
            return plan.get((i, k))

        def before(i, k):
            return (i, k - 1) if k else (i - 1, NU - 1)

        def tile_of(i, k):
            return c.tiles_before[plan[i, k]]

        with nc.Block() as block:
            @block.sync
            def _(sp):
                for n in range(first, c.next_unit + 2):
                    load_unit(c, sp, n)

            @block.gpsimd
            def _(pool):
                pool.memset(xph[:, :, :, 64:128].bitcast(F32), 0.0).then_inc(s_clear, 1)
                pool.memset(xpl[:, :, :, 64:128].bitcast(F32), 0.0).then_inc(s_clear, 1)

                def complete(g, p):
                    base = 6 * g + 3 * p
                    for d, a in ((0, slice(P, T)), (1, slice(0, T - P))):
                        pool.wait_ge(s_asm, base + 2 + d)
                        if d:
                            pool.wait_ge(s_fin, base + 1)
                        pool.tensor_tensor(y[:, p, a], y[:, p, a], parts[:, d * (T - P):(d + 1) * (T - P)],
                                           ALU.add).then_inc(s_fin, 1)
                    pool.wait_ge(s_fin, base + 2)
                    pool.wait_ge(s_zsilu, g + 1)
                    pool.tensor_tensor(y[:, p, :], y[:, p, :], zs[:, g % 2, p, :], ALU.mult).then_inc(s_fin, 1)

                for i, k in slots:
                    g = i - 1
                    if k == 0 and i - 2 in G:
                        complete(i - 2, 1)
                    if g not in G:
                        continue
                    if k == 7:
                        complete(g, 0)
                    if k == 1:
                        if g:
                            pool.wait_ge(s_e, 4 * g)
                        for p in range(2):
                            for d in range(2):
                                pool.affine_select(
                                    out=pick[:, 2 * p + d, :].rearrange("r (h m) -> r h m", h=2),
                                    in_=c.ones[0:64, :].rearrange("r (h m) -> r h m", h=2),
                                    compare_op=ALU.is_equal, fill=0.0, base=-(HPG * g + 2 * p + SH * d),
                                    pattern=[[-1, 2], [0, 64]], channel_multiplier=1).then_inc(s_pick, 1)
                    if 2 <= k <= 5:
                        t = k - 2
                        pool.wait_ge(s_cbm, 2 * g + 2)
                        if g or t:
                            pool.wait_ge(s_m, 3 * (4 * g + t) - 1)
                        if t == 0:
                            pool.wait_ge(s_xwl, g + 1)
                        pool.tensor_tensor(t2.rearrange("p (h l) -> p h l", h=HPG),
                                           again(cbm[:, 1, t * P:(t + 1) * P], HPG),
                                           spread(head(dtc, 1, t, g), P), ALU.mult).then_inc(s_t2, 1)
                    if 1 <= k <= 4:
                        t = k - 1
                        if g or t:
                            pool.wait_ge(s_arg, 4 * g + t)
                        for j, (part, mask, d) in enumerate(((lah, c.ge, 0), (lal, c.ge, 0),
                                                             (lah, c.le, 1), (lal, c.le, 1))):
                            pool.tensor_tensor(rhs[:, j, :, :], again(mask[:, :], HPG),
                                               spread(head(part, d, t, g), P), ALU.mult).then_inc(s_rhs, 1)

            @block.tensor
            def _(pe):
                def decay_sums(g, t):
                    i = 4 * g + t
                    pe.wait_ge(s_rhs, 4 * (i + 1))
                    if t == 0 and g:
                        pe.wait_ge(s_ee, 4 * g)
                    if t:
                        pe.wait_ge(s_decay, i)
                    flat = lambda j: rhs[:, j, :, :].rearrange("p h l -> p (h l)")
                    pe.matmul(q[4][:, :], c.gt_r[:, :], flat(0), start=True, stop=False)
                    pe.matmul(q[4][:, :], c.gt_r[:, :], flat(1), start=False, stop=False)
                    pe.matmul(q[4][:, :], c.lt_r[:, :], flat(2), start=False, stop=False)
                    pe.matmul(q[4][:, :], c.lt_r[:, :], flat(3), start=False, stop=True).then_inc(s_arg, 1)

                def spread_cum(g, e):
                    p, d = e // 2, e % 2
                    dst = q[0] if e == 3 else q[4]
                    if e == 0:
                        pe.wait_ge(s_pick, 4 * g + 4)
                        pe.wait_ge(s_decay, 4 * g + 4)
                    elif e < 3:
                        pe.wait_ge(s_ee, 4 * g + e)
                    else:
                        pe.wait_ge(s_asm, 6 * g + 3)
                    w = pick[:, e, :]
                    pe.matmul(dst[:, :], w, cum_h[:, :], start=True, stop=False)
                    pe.matmul(dst[:, :], w, cum_l[:, :], start=False, stop=True).then_inc(s_e, 1)

                def y_intra(g, t):
                    pe.wait_ge(s_ml, 4 * g + t + 1)
                    if t == 0:
                        pe.wait_ge(s_xpl, 5 * g + 5)
                        pe.wait_ge(s_xw, 4 * g + 4)
                    for p in range(2):
                        for h in range(2):
                            a = slice(64 * h, 64 * h + P)
                            last = mm3(pe, q[p][:, t * P:(t + 1) * P], xph[:, t, p, a], xpl[:, t, p, a],
                                       mh[:, 2 * p + h, :], ml[:, 2 * p + h, :], h == 0, h == 1, skip=True)
                    last.then_inc(s_y, 1)

                def contributions(g, j):
                    if j == 0:
                        pe.wait_ge(s_xwl, g + 1)
                        pe.wait_ge(s_xpl, 5 * g + 5)
                    if j == 1:
                        pe.wait_ge(s_cbm, 2 * g + 2)
                        if g:
                            pe.wait_ge(s_rs, 2 * g - 1)
                    if j == 2:
                        pe.wait_ge(s_st, 7 * g + 1)
                    dst = q[2 + j % 2]
                    for d, t in ((0, j), (1, NT - 1 - j)):
                        b = slice(t * P, (t + 1) * P)
                        jj = j if d == 0 else 2 - j
                        last = mm3(pe, dst[:, d * GW:(d + 1) * GW], bth[:, b], btl[:, b], xwh[:, d, jj, :],
                                   xwl[:, d, jj, :], True, True)
                    last.then_inc(s_con, 1)

                def y_inter(g, p):
                    if p == 0:
                        pe.wait_ge(s_sl, 3 * g + 3)
                        pe.wait_ge(s_st, 7 * g + 7)
                    else:
                        pe.wait_ge(s_asm, 6 * g + 3)
                    for d in range(2):
                        for t in (range(1, NT) if d == 0 else range(NT - 1)):
                            j = t - 1 if d == 0 else 2 - t
                            a = slice(d * GW + p * P, d * GW + (p + 1) * P)
                            b = slice(t * P, (t + 1) * P)
                            last = mm3(pe, q[2 + d][:, b], sth[:, j, a], stl[:, j, a], bch[:, 1, b], bcl[:, 1, b],
                                       True, True)
                    last.then_inc(s_int, 1)

                for i, k in slots:
                    g, f = i - 1, i - 2
                    n = unit_in(i, k)
                    if n is not None:
                        if k == 4:
                            pe.wait_ge(s_yl, f + 1)
                        if k in (4, 7):
                            stream_products(c, pe, n, lambda j: yh[:, j, :], lambda j: yl[:, j, :])
                        else:
                            stream_products(c, pe, n, lambda j: c.uh[:, j, :], lambda j: c.ul[:, j, :])
                    if k == 1 and f in G:
                        pe.wait_ge(s_sq, 2 * f + 2)
                        if g in G:
                            pe.wait_ge(s_cbm, 2 * g + 2)
                        for p in range(2):
                            last = pe.matmul(q[3][:, :], c.ones[:, :], ex[:, p, :], start=p == 0, stop=p == 1)
                        last.then_inc(s_nrm, 1)
                    if g not in G:
                        continue
                    if k == 0:
                        pe.wait_ge(s_silu, g + 1)
                        if g:
                            pe.wait_ge(s_asm, 6 * g)
                            pe.wait_ge(s_ee, 4 * g)
                        for t in range(NT):
                            for j in range(2):
                                a = (t % 2) * GW + j * P
                                pe.transpose(q[t // 2][:, a:a + P], xt[:, g % 2, j, t * P:(t + 1) * P],
                                             c.ident[:, :])
                        for t in range(NT):
                            last = pe.transpose(q[2][:, t * P:(t + 1) * P], bct[:, 0, t * P:(t + 1) * P],
                                                c.ident[:, :])
                        last.then_inc(s_tx, 1)
                        pe.wait_ge(s_bcl, g + 1)
                        for t in range(NT):
                            b = slice(t * P, (t + 1) * P)
                            last = mm3(pe, q[3][:, b], bch[:, 0, b], bcl[:, 0, b], bch[:, 1, b], bcl[:, 1, b],
                                       True, True)
                        last.then_inc(s_cb, 1)
                    if 2 <= k <= 4:
                        contributions(g, k - 2)
                    if 2 <= k <= 5:
                        y_intra(g, k - 2)
                    if 1 <= k <= 4:
                        decay_sums(g, k - 1)
                    if k == 5:
                        spread_cum(g, 0)
                    if k == 6:
                        y_inter(g, 0)
                        spread_cum(g, 1)
                    if k == 7:
                        spread_cum(g, 2)
                        y_inter(g, 1)
                        spread_cum(g, 3)

            @block.scalar
            def _(act):
                act.preload_act_table_set(LN_EXP)
                for n in range(first, first + 2):
                    split_hi(c, act, n)
                for i, k in slots:
                    g, f = i - 1, i - 2
                    pi, pk = before(i, k)
                    if (pi, pk) in plan and pk in CONV:
                        cj = CONV[pk]
                        t, ct = tile_of(pi, pk), conv_tile(pi, cj)
                        act.wait_ge(c.tile_done, t + 1)
                        if cj >= 2 and pi:
                            act.wait_ge(s_tx, pi)
                        if cj < 2 and pi >= 2:
                            act.wait_ge(s_asm, 6 * (pi - 1))
                        act.activation(conv_out(pi, cj), bank(c, t)[:, :], ACT.Identity, scale=tap(2, ct),
                                       bias=par[:, at["ssd_conv_b"] + ct:at["ssd_conv_b"] + ct + 1])\
                           .then_inc(s_center, 1)
                    if (pi, pk) in plan and pk in (0, 1):
                        t = tile_of(pi, pk)
                        act.wait_ge(c.tile_done, t + 1)
                        if pi >= 2:
                            act.wait_ge(s_fin, 6 * (pi - 1))
                        act.activation(zs[:, pi % 2, pk, :], bank(c, t)[:, :], ACT.Copy)\
                           .then_inc(c.bank_free[t % SB], 1)
                    if unit_in(i, k) is not None:
                        split_hi(c, act, unit_in(i, k) + 2)
                    if k in (6, 7) and g in G:
                        e = k - 6
                        act.wait_ge(s_e, 4 * g + e + 1)
                        if e == 0 and g:
                            act.wait_ge(s_nrm, g)
                        act.activation(ex[:, e, :], q[4][:, :], ACT.Exp).then_inc(s_ee, 1)
                    if k == 0 and f in G:
                        for e in (2, 3):
                            act.wait_ge(s_e, 4 * f + e + 1)
                            act.wait_ge(s_asm, 6 * f + 3)
                            act.activation(ex[:, e - 2, :], q[4 if e == 2 else 0][:, :], ACT.Exp).then_inc(s_ee, 1)
                    if k == 0 and g in G:
                        act.wait_ge(s_silu, g + 1)
                        if g:
                            act.wait_ge(s_int, 2 * g)
                        act.activation(bch[:, :, :], bct[:, :, :], ACT.Copy).then_inc(s_bch, 1)
                    if k == 0 and f in G:
                        act.wait_ge(s_fin, 6 * f + 6)
                        act.wait_ge(s_asm, 6 * f + 6)
                        for p in range(2):
                            act.activation(ex[:, p, :], y[:, p, :], ACT.Square).then_inc(s_sq, 1)
                    if k == 1 and g in G:
                        act.wait_ge(s_tx, g + 1)
                        act.wait_ge(s_clear, 2)
                        if g:
                            act.wait_ge(s_y, 4 * g)
                        for b in range(2):
                            for h in range(2):
                                src = q[b][:, :].rearrange("p (t j h m) -> p t j h m", t=2, j=2, h=2)[:, :, :, h, :]
                                act.activation(xph[:, 2 * b:2 * b + 2, :, P * h:P * h + 64], src, ACT.Copy)\
                                   .then_inc(s_xph, 1)
                        if g:
                            act.wait_ge(s_con, 3 * g)
                        act.activation(bth[:, :], q[2][:, :], ACT.Copy).then_inc(s_xph, 1)
                        act.wait_ge(s_xw, 4 * g + 4)
                        act.activation(xwh[:, :, :, :], xwf, ACT.Copy).then_inc(s_xwh, 1)
                    if k == 2 and f in G:
                        act.wait_ge(s_nrm, f + 1)
                        act.activation(rstd, q[3][:, :], ACT.Ln, scale=1.0 / GW, bias=c.eps[:, 0:1])\
                           .then_inc(s_rs, 1)
                        act.wait_ge(s_rs, 2 * f + 1)
                        act.activation(rstd, rstd, ACT.Exp, scale=-0.5).then_inc(s_rs, 1)
                    if 2 <= k <= 5 and g in G:
                        t = k - 2
                        act.wait_ge(s_arg, 4 * g + t + 1)
                        if t == 0:
                            act.wait_ge(s_xwl, g + 1)
                        else:
                            act.wait_ge(s_m, 3 * (4 * g + t))
                        act.activation(decay, q[4][:, :], ACT.Exp).then_inc(s_decay, 1)
                        act.wait_ge(s_m, 3 * (4 * g + t + 1))
                        if g or t:
                            act.wait_ge(s_y, 4 * g + t)
                        act.activation(mh[:, :, :], t1.rearrange("p (h l) -> p h l", h=HPG), ACT.Copy)\
                           .then_inc(s_mh, 1)
                    if k == 2 and f in G:
                        act.wait_ge(s_yn, 2 * f + 2)
                        if f:
                            act.wait_ge(c.tile_done, c.tiles_before[plan[f + 1, 7] + 1])
                        act.activation(yh[:, :, :], y[:, :, :], ACT.Copy).then_inc(s_yh, 1)
                    if 3 <= k <= 5 and g in G:
                        j = k - 3
                        act.wait_ge(s_st, 7 * g + 1 + 3 * j)
                        if j == 0 and g:
                            act.wait_ge(s_int, 2 * g)
                        act.activation(sth[:, j, :], st[:, :, :].rearrange("p d m -> p (d m)"), ACT.Copy)\
                           .then_inc(s_sh, 1)
                    if k == 7:
                        if i in G:
                            for j in CONV:
                                act.wait_ge(*free_value(c, tile_of(i, j)))
                            act.activation(xt[:, i % 2, :, :], xt[:, i % 2, :, :], ACT.Silu)
                            act.activation(bct[:, :, :], bct[:, :, :], ACT.Silu).then_inc(s_silu, 1)
                        if g in G:
                            act.wait_ge(*free_value(c, tile_of(g, 1)))
                            act.activation(zs[:, g % 2, :, :], zs[:, g % 2, :, :], ACT.Silu).then_inc(s_zsilu, 1)
                        if i < NI - 1:
                            act.preload_act_table_set(LN_EXP)

            @block.vector
            def _(dve):
                for n in range(first, first + 2):
                    split_lo(c, dve, n)
                taps = [0]

                def close(i, k, j):
                    t, m = tile_of(i, k) + j, (k - 4) // 3 * 4 + j
                    dve.wait_ge(c.tile_done, t + 1)
                    if i > 2:
                        dve.wait_ge(*free_value(c, tile_of(i - 1, k) + j))
                    dve.tensor_tensor(c.h[:, m, :], c.h[:, m, :], bank(c, t)[:, :], ALU.add)\
                       .then_inc(c.bank_free[t % SB], 1)

                def assemble(g, p):
                    base = 6 * g + 3 * p
                    dve.wait_ge(s_y, 4 * g + 4)
                    dve.wait_ge(s_int, 2 * g + p + 1)
                    dve.wait_ge(s_ee, 4 * g + 2 * p + 2)
                    if base:
                        dve.wait_ge(s_fin, base)
                    if g:
                        dve.wait_ge(s_yh, g)
                    col = at["ssd_d"] + 2 * g + p
                    dve.scalar_tensor_tensor(out=y[:, p, :], in0=xt[:, g % 2, p, :], scalar=par[:, col:col + 1],
                                             in1=q[p][:, :], op0=ALU.mult, op1=ALU.add).then_inc(s_asm, 1)
                    for d, a in ((0, slice(P, T)), (1, slice(0, T - P))):
                        dve.tensor_tensor(parts[:, d * (T - P):(d + 1) * (T - P)], q[2 + d][:, a], ex[:, d, a], ALU.mult)\
                           .then_inc(s_asm, 1)

                for i, k in slots:
                    g, f = i - 1, i - 2
                    pi, pk = before(i, k)
                    if (pi, pk) in plan and pk in CONV:
                        cj = CONV[pk]
                        t, ct = tile_of(pi, pk), conv_tile(pi, cj)
                        dve.wait_ge(s_center, 4 * pi + cj + 1)
                        dst, src = conv_out(pi, cj), bank(c, t)
                        for tp, last in ((0, 0), (1, 0), (3, 0), (4, 1)):
                            o = tp - 2
                            a, b = max(0, -o), T - max(0, o)
                            ins = dve.scalar_tensor_tensor(out=dst[:, a:b], in0=src[:, a + o:b + o],
                                                           scalar=tap(tp, ct), in1=dst[:, a:b], op0=ALU.mult,
                                                           op1=ALU.add)
                            if last:
                                ins.then_inc(c.bank_free[t % SB], 1)
                            else:
                                ins.then_inc(s_tap, 1)
                                taps[0] += 1
                                dve.wait_ge(s_tap, taps[0])
                    if (pi, pk) in plan and pk in (4, 7):
                        for j in range(1, 4):
                            close(pi, pk, j)
                    if unit_in(i, k) is not None:
                        split_lo(c, dve, unit_in(i, k) + 2)
                        if k in (4, 7):
                            close(i, k, 0)
                    if k == 0 and f in G:
                        assemble(f, 1)
                    if k == 0 and g in G:
                        dve.wait_ge(s_bch, g + 1)
                        dve.tensor_tensor(bcl[:, :, :], bct[:, :, :], bch[:, :, :].bitcast(F32), ALU.subtract)\
                           .then_inc(s_bcl, 1)
                    if k == 1 and g in G:
                        if g:
                            dve.wait_ge(s_t2, 4 * g)
                        dve.wait_ge(s_cb, g + 1)
                        for d, mask in ((0, c.ge), (1, c.le)):
                            dve.tensor_tensor(cbm[:, d, :].rearrange("p (t l) -> p t l", t=NT),
                                              q[3][:, :].rearrange("p (t l) -> p t l", t=NT),
                                              again(mask[:, :], NT), ALU.mult).then_inc(s_cbm, 1)
                        dve.wait_ge(s_xph, 5 * g + 5)
                        for b in range(2):
                            for h in range(2):
                                src = q[b][:, :].rearrange("p (t j h m) -> p t j h m", t=2, j=2, h=2)[:, :, :, h, :]
                                a = slice(P * h, P * h + 64)
                                dve.tensor_tensor(xpl[:, 2 * b:2 * b + 2, :, a], src,
                                                  xph[:, 2 * b:2 * b + 2, :, a].bitcast(F32), ALU.subtract)\
                                   .then_inc(s_xpl, 1)
                        dve.tensor_tensor(btl[:, :], q[2][:, :], bth[:, :].bitcast(F32), ALU.subtract)\
                           .then_inc(s_xpl, 1)
                        if g:
                            dve.wait_ge(s_ml, 4 * g)
                        for d, t0, nt in ((0, 0, 2), (0, 2, 1), (1, 1, 1), (1, 2, 2)):
                            src = q[t0 // 2][:, (t0 % 2) * GW:(t0 % 2 + nt) * GW]
                            w = wc[:, t0:t0 + nt, 32 * d + HPG * g:32 * d + HPG * (g + 1)]
                            for u in range(nt):
                                ins = dve.tensor_tensor(
                                    xwf[:, d, t0 - d + u, :].rearrange("p (h m) -> p h m", h=HPG),
                                    src[:, u * GW:(u + 1) * GW].rearrange("p (h m) -> p h m", h=HPG),
                                    spread(w[:, u, :], HD), ALU.mult)
                            ins.then_inc(s_xw, 1)
                        dve.wait_ge(s_xwh, g + 1)
                        dve.tensor_tensor(xwl[:, :, :, :], xwf, xwh[:, :, :, :].bitcast(F32), ALU.subtract)\
                           .then_inc(s_xwl, 1)
                    if 2 <= k <= 5 and g in G:
                        t = k - 2
                        m = 3 * (4 * g + t)
                        v = t1.rearrange("p (h l) -> p h l", h=HPG)
                        if t == 0:
                            dve.wait_ge(s_xwl, g + 1)
                        else:
                            dve.wait_ge(s_ml, 4 * g + t)
                        dve.tensor_tensor(v, again(cbm[:, 0, t * P:(t + 1) * P], HPG),
                                          spread(head(dtc, 0, t, g), P), ALU.mult).then_inc(s_m, 1)
                        dve.wait_ge(s_m, m + 1)
                        dve.wait_ge(s_t2, 4 * g + t + 1)
                        dve.tensor_tensor(t1, t1, t2, ALU.add).then_inc(s_m, 1)
                        dve.wait_ge(s_m, m + 2)
                        dve.wait_ge(s_decay, 4 * g + t + 1)
                        dve.tensor_tensor(t1, t1, decay, ALU.mult).then_inc(s_m, 1)
                        dve.wait_ge(s_mh, 4 * g + t + 1)
                        dve.tensor_tensor(ml[:, :, :], v, mh[:, :, :].bitcast(F32), ALU.subtract)\
                           .then_inc(s_ml, 1)
                    if 3 <= k <= 5 and g in G:
                        j = k - 3
                        dve.wait_ge(s_con, 3 * g + j + 1)
                        flat = st[:, :, :].rearrange("p d m -> p (d m)")
                        if j == 0:
                            dve.tensor_copy(flat, q[2][:, :]).then_inc(s_st, 1)
                        else:
                            for d, t in ((0, j), (1, NT - 1 - j)):
                                s4 = st[:, d, :].rearrange("p (h m) -> p h m", h=HPG)
                                dve.tensor_tensor(s4, s4, spread(head(et, d, t, g), HD), ALU.mult).then_inc(s_st, 1)
                            dve.wait_ge(s_st, 7 * g + 3 * j)
                            dve.tensor_tensor(flat, flat, q[2 + j % 2][:, :], ALU.add).then_inc(s_st, 1)
                        dve.wait_ge(s_sh, 3 * g + j + 1)
                        dve.tensor_tensor(stl[:, j, :], flat, sth[:, j, :].bitcast(F32), ALU.subtract)\
                           .then_inc(s_sl, 1)
                    if k == 2 and f in G:
                        dve.wait_ge(s_rs, 2 * f + 2)
                        for p in range(2):
                            col = at["ssd_gnorm"] + 2 * f + p
                            dve.scalar_tensor_tensor(out=y[:, p, :], in0=y[:, p, :], scalar=par[:, col:col + 1],
                                                     in1=rstd, op0=ALU.mult, op1=ALU.mult).then_inc(s_yn, 1)
                        dve.wait_ge(s_yh, f + 1)
                        dve.tensor_tensor(yl[:, :, :], y[:, :, :], yh[:, :, :].bitcast(F32), ALU.subtract)\
                           .then_inc(s_yl, 1)
                    if k == 7 and g in G:
                        assemble(g, 0)


GLA_SLOTS = 14


def gla_units(c, A):
    w_in, w_out = A["gla_w_in"][0], A["gla_w_out"][0]
    QK = GH * P
    NU = GLA_SLOTS
    plan, n = {}, len(c.units)
    for i in range(GH + 1):
        for k in range(NU):
            closes = k >= 10
            g = i - 1 if closes else i
            if not 0 <= g < GH:
                continue
            if closes:
                a = (k - 10) * 256
                add_units(c, [w_out[g * GV:(g + 1) * GV, a:a + 256].rearrange("(k p) m -> p k m", p=P)], 2)
            else:
                col = (g * P if k == 0 else QK + g * P if k == 1 else
                       2 * QK + g * GV + (k - 2) * P if k < 6 else 2 * QK + SI + g * GV + (k - 6) * P)
                add_units(c, [w_in[:, col:col + P].rearrange("(k p) m -> p k m", p=P)], 1)
            plan[i, k] = n
            n += 1
    return plan


def gla_stage(nc, c, A, plan):
    par, at = c.par, c.at
    w_in = A["gla_w_in"][0]
    QK = GH * P
    NU = GLA_SLOTS
    slots = [(i, k) for i in range(GH + 1) for k in range(NU)] + [(GH + 1, 0)]
    first = c.next_unit
    c.next_unit = first + len(plan)
    STEPS = [(0, 0), (1, NT - 1), (0, 1), (1, NT - 2), (0, 2), (1, NT - 3)]

    with ExitStack() as ctx:
        sb = lambda n, s, d=F32: ctx.enter_context(nc.sbuf_tensor("gla_" + n, s, d))
        sem = stage_semaphores(nc, ctx, "gla_")
        glt = sb("gl", [32, T])
        wg = sb("w_gates", [32, 2, GH * P])
        go = sb("restart", [P, 2, T])
        s_gl = {n: sem("gl_" + n) for n in ("w", "zero", "u", "mm", "out", "go")}
        with ExitStack() as pre:
            pb = lambda n, s, d=F32: pre.enter_context(nc.sbuf_tensor("gla_" + n, s, d))
            wgl = pb("wgl", [P, KT, 32])
            una = pb("u", [P, 2, T])
            with nc.Block() as block:
                @block.sync
                def _(sp):
                    sp.dma_start(wgl[:, :, :], w_in[:, 2 * QK + 2 * SI:2 * QK + 2 * SI + 32]
                                 .rearrange("(k p) m -> p k m", p=P)).then_inc(s_gl["w"], 16)
                    sp.wait_ge(s_gl["zero"], 1)
                    for d in range(2):
                        sp.dma_start(wg[16 * d:16 * d + 16, d, :], A["gla_w_gate"][0][d]).then_inc(s_gl["w"], 16)

                @block.gpsimd
                def _(pool):
                    pool.memset(wg[:, :, :], 0.0).then_inc(s_gl["zero"], 1)
                    pool.memset(go[:, :, :], 1.0).then_inc(s_gl["go"], 1)
                    pool.wait_ge(s_gl["go"], 1)
                    pool.memset(go[:, 0, 0:T:P], 0.0).then_inc(s_gl["go"], 1)
                    pool.memset(go[:, 1, P - 1:T:P], 0.0).then_inc(s_gl["go"], 1)

                @block.tensor
                def _(pe):
                    pe.wait_ge(s_gl["w"], 48)
                    for k in range(KT):
                        pe.wait_ge(s_gl["u"], k + 1)
                        pe.matmul(c.q[0][0:32, :], wgl[:, k, :], una[:, k % 2, :], start=k == 0,
                                  stop=k == KT - 1).then_inc(s_gl["mm"], 1)

                @block.vector
                def _(dve):
                    for k in range(KT):
                        if k >= 2:
                            dve.wait_ge(s_gl["mm"], k - 1)
                        dve.tensor_tensor(una[:, k % 2, :], c.uh[:, k, :].bitcast(F32),
                                          c.ul[:, k, :].bitcast(F32), ALU.add).then_inc(s_gl["u"], 1)
                    dve.wait_ge(s_gl["mm"], KT)
                    dve.tensor_copy(glt[:, :], c.q[0][0:32, :]).then_inc(s_gl["out"], 1)

        lg = sb("log_gate", [P, 2, T])
        ep = sb("q_gated", [P, 2, T])
        em = sb("k_gated", [P, 2, T])
        qs, ks = sb("q", [P, T]), sb("k", [P, T])
        mid, tot, dif = sb("middle", [P, 2, NT]), sb("total", [P, 2, NT]), sb("rest", [P, 2, NT])
        qh, ql = sb("q_hi", [P, 2, T], F32R), sb("q_lo", [P, 2, T], F32R)
        kh, kl = sb("k_hi", [P, 2, T], F32R), sb("k_lo", [P, 2, T], F32R)
        att = sb("att", [P, 2, T])
        ath, atl = sb("att_hi", [P, T], F32R), sb("att_lo", [P, T], F32R)
        vf = sb("v", [P, T])
        vh, vl = sb("v_hi", [P, NT, GV], F32R), sb("v_lo", [P, NT, GV], F32R)
        st = sb("state", [P, 2, GV])
        sth, stl = sb("state_hi", [P, 2, GV], F32R), sb("state_lo", [P, 2, GV], F32R)
        con = sb("contribution", [P, T])
        o = sb("o", [P, NT, GV])
        ssq, rstd = sb("square_sums", [P, NT]), sb("rstd", [P, NT])
        zs = sb("z", [P, 4, T])
        yh, yl = sb("y_hi", [P, 4, T], F32R), sb("y_lo", [P, 4, T], F32R)
        q = c.q
        (s_zero, s_gate, s_act, s_lg, s_cen, s_small, s_e, s_kc, s_qc, s_g, s_hi, s_lo, s_att, s_kt, s_kth, s_ktl,
         s_am, s_ath, s_atl, s_vt, s_vth, s_vtl, s_con, s_cs, s_st, s_sth, s_stl, s_in, s_sq, s_rs, s_on,
         s_ot, s_y, s_yh, s_yl, s_z) = (sem(n) for n in (
             "cleared", "gate_products", "gate_act", "log_gates", "centred", "ends", "decays", "k_copied",
             "q_copied", "gated", "qk_rounded", "qk_rest", "att_products", "k_transposed", "k_tok_rounded",
             "k_tok_rest", "att_masked", "att_rounded", "att_rest", "v_transposed", "v_rounded",
             "v_rest", "contributions", "con_scaled", "states", "state_rounded", "state_rest", "o_products",
             "squared", "rstd_ready", "o_normed", "o_transposed", "y_parts", "y_rounded", "y_rest", "silu_done"))
        G = range(GH)

        def unit_in(i, k):
            return plan.get((i, k))

        def before(i, k):
            return (i, k - 1) if k else (i - 1, NU - 1)

        def tile_of(i, k):
            return c.tiles_before[plan[i, k]]

        with nc.Block() as block:
            @block.sync
            def _(sp):
                for n in range(first, c.next_unit + 2):
                    load_unit(c, sp, n)

            @block.gpsimd
            def _(pool):
                pool.memset(att[:, :, :], 0.0).then_inc(s_zero, 1)
                add_squares(c, pool)

            @block.tensor
            def _(pe):
                def contribution(g, j):
                    d, t = STEPS[j]
                    m = 6 * g + j
                    if j == 0:
                        pe.wait_ge(s_vtl, 4 * g + 4)
                        pe.wait_ge(s_ktl, 2 * g + 2)
                    else:
                        pe.wait_ge(s_cs, m)
                    b = slice(t * P, (t + 1) * P)
                    mm3(pe, q[4][:, :], kh[:, d, b], kl[:, d, b], vh[:, t, :], vl[:, t, :], True, True)\
                        .then_inc(s_con, 1)

                def inter(g, j):
                    d, t = STEPS[j]
                    t += 1 if d == 0 else -1
                    pe.wait_ge(s_stl, 6 * g + j + 1)
                    b = slice(t * P, (t + 1) * P)
                    done = not any(e != d and u + (1 if e == 0 else -1) == t for e, u in STEPS[j + 1:])
                    mm3(pe, q[t][:, :], qh[:, d, b], ql[:, d, b], sth[:, d, :], stl[:, d, :], False, done,
                        skip=True).then_inc(s_in, 1)

                for i, k in slots:
                    g, f = i, i - 1
                    n = unit_in(i, k)
                    if n is not None:
                        if k == 10:
                            pe.wait_ge(s_yl, f + 1)
                        if k >= 10:
                            stream_products(c, pe, n, lambda j: yh[:, j, :], lambda j: yl[:, j, :])
                        else:
                            stream_products(c, pe, n, lambda j: c.uh[:, j, :], lambda j: c.ul[:, j, :])
                    if k < 2 and f in G:
                        pe.wait_ge(s_on, 4 * f + 4)
                        if k == 1:
                            pe.wait_ge(s_y, 4 * f + 2)
                        for j in (2 * k, 2 * k + 1):
                            for t in range(NT):
                                last = pe.transpose(q[2 + j % 2][:, t * P:(t + 1) * P],
                                                    o[:, t, j * P:(j + 1) * P], c.ident[:, :])
                        last.then_inc(s_ot, 1)
                    if g not in G:
                        continue
                    if k == 0:
                        if g:
                            pe.wait_ge(s_on, 4 * g)
                        for d in range(2):
                            last = pe.matmul(q[d][:, :], wg[:, d, g * P:(g + 1) * P], glt[:, :], start=True,
                                             stop=True)
                        last.then_inc(s_gate, 1)
                    if 3 <= k <= 6:
                        j = k - 3
                        pe.wait_ge(*free_value(c, tile_of(g, 2 + j)))
                        if j:
                            pe.wait_ge(s_vtl, 4 * g + j)
                        elif g:
                            pe.wait_ge(s_cs, 6 * g)
                        for t in range(NT):
                            last = pe.transpose(q[4][:, t * P:(t + 1) * P], vf[:, t * P:(t + 1) * P],
                                                c.ident[:, :])
                        last.then_inc(s_vt, 1)
                    if k == 3:
                        pe.wait_ge(s_lo, 4 * g + 4)
                        pe.wait_ge(s_lg, 6 * g + 6)
                        if g:
                            pe.wait_ge(s_y, 4 * g)
                        for d in range(2):
                            for t in range(NT):
                                b = slice(t * P, (t + 1) * P)
                                last = mm3(pe, q[d][:, b], kh[:, d, b], kl[:, d, b], qh[:, d, b], ql[:, d, b],
                                           True, True)
                        last.then_inc(s_att, 1)
                        for d in range(2):
                            for t in range(NT):
                                last = pe.transpose(q[2 + d][:, t * P:(t + 1) * P], em[:, d, t * P:(t + 1) * P],
                                                    c.ident[:, :])
                        last.then_inc(s_kt, 1)
                    if k == 7:
                        contribution(g, 0)
                        pe.wait_ge(s_atl, g + 1)
                        for t in range(NT):
                            b = slice(t * P, (t + 1) * P)
                            mm3(pe, q[t][:, :], ath[:, b], atl[:, b], vh[:, t, :], vl[:, t, :], True, False,
                                skip=True)
                    if 8 <= k <= 13:
                        if k < 13:
                            contribution(g, k - 7)
                        inter(g, k - 8)

            @block.scalar
            def _(act):
                act.preload_act_table_set(LN_EXP)
                for n in range(first, first + 2):
                    split_hi(c, act, n)
                for i, k in slots:
                    g, f = i, i - 1
                    pi, pk = before(i, k)
                    if (pi, pk) in plan and pk < 10:
                        t = tile_of(pi, pk)
                        act.wait_ge(c.tile_done, t + 1)
                        inc = (c.bank_free[t % SB], 1)
                        if pk == 0:
                            if pi:
                                act.wait_ge(s_g, 4 * pi)
                            act.activation(qs[:, :], bank(c, t)[:, :], ACT.Copy, scale=float(P) ** -0.5)\
                               .then_inc(*inc)
                        elif pk == 1:
                            if pi:
                                act.wait_ge(s_g, 4 * pi)
                            act.activation(ks[:, :], bank(c, t)[:, :], ACT.Copy).then_inc(*inc)
                        elif pk < 6:
                            if pk > 2 or pi:
                                act.wait_ge(s_vt, 4 * pi + pk - 2)
                            act.activation(vf[:, :], bank(c, t)[:, :], ACT.Copy).then_inc(*inc)
                        else:
                            if pk == 6 and pi:
                                act.wait_ge(s_yh, pi)
                                act.wait_ge(s_yl, pi)
                            act.activation(zs[:, pk - 6, :], bank(c, t)[:, :], ACT.Copy).then_inc(*inc)
                    if unit_in(i, k) is not None:
                        split_hi(c, act, unit_in(i, k) + 2)
                    if pi == GH and pk >= 10:
                        for j in range(2):
                            square_tile(c, act, (pk - 10) * 2 + j, free_value(c, tile_of(pi, pk) + j))
                    if k == 0 and f in G:
                        act.wait_ge(s_in, 6 * f + 6)
                        for t in range(NT):
                            if f or t:
                                act.wait_ge(s_sq, 4 * f + t)
                            act.activation(con[:, :], q[t][:, :], ACT.Square, accum_out=ssq[:, t:t + 1])\
                               .then_inc(s_sq, 1)
                        act.wait_ge(s_sq, 4 * f + 4)
                        act.activation(rstd[:, :], ssq[:, :], ACT.Ln, scale=1.0 / GV, bias=c.eps[:, 0:1])\
                           .then_inc(s_rs, 1)
                        act.wait_ge(s_rs, 2 * f + 1)
                        act.activation(rstd[:, :], rstd[:, :], ACT.Exp, scale=-0.5).then_inc(s_rs, 1)
                    if k == 1 and g in G:
                        act.wait_ge(s_gate, g + 1)
                        if g:
                            act.wait_ge(s_kt, g)
                        for d in range(2):
                            b = par[:, at["gla_b_gate"] + 4 * d + g:at["gla_b_gate"] + 4 * d + g + 1]
                            act.activation(em[:, d, :], q[d][:, :], ACT.Abs, bias=b).then_inc(s_act, 1)
                            act.wait_ge(s_act, 6 * g + 3 * d + 1)
                            act.activation(em[:, d, :], em[:, d, :], ACT.Exp, scale=-1.0).then_inc(s_act, 1)
                            act.wait_ge(s_act, 6 * g + 3 * d + 2)
                            act.activation(em[:, d, :], em[:, d, :], ACT.Ln, bias=1.0).then_inc(s_act, 1)
                    if k == 2 and g in G:
                        act.wait_ge(s_cen, 5 * g + 5)
                        act.activation(ep[:, :, :], lg[:, :, :], ACT.Exp, scale=1.0 / 16).then_inc(s_e, 1)
                        act.activation(em[:, :, :], lg[:, :, :], ACT.Exp, scale=-1.0 / 16).then_inc(s_e, 1)
                        for b in (mid, tot, dif):
                            act.activation(b[:, :, :], b[:, :, :], ACT.Exp, scale=1.0 / 16).then_inc(s_e, 1)
                        act.wait_ge(s_g, 4 * g + 4)
                        if g:
                            act.wait_ge(s_in, 6 * g)
                        act.activation(qh[:, :, :], ep[:, :, :], ACT.Copy).then_inc(s_hi, 1)
                        act.activation(kh[:, :, :], em[:, :, :], ACT.Copy).then_inc(s_hi, 1)
                    if k == 4 and f in G:
                        act.wait_ge(s_y, 4 * f + 4)
                        if f:
                            act.wait_ge(c.tile_done, c.tiles_before[plan[f, 13] + 1])
                        act.activation(yh[:, :, :], zs[:, :, :], ACT.Copy).then_inc(s_yh, 1)
                    if 4 <= k <= 7 and g in G:
                        j = k - 4
                        act.wait_ge(s_vt, 4 * g + j + 1)
                        if j == 0 and g:
                            act.wait_ge(s_con, 6 * g)
                        act.activation(vh[:, :, j * P:(j + 1) * P], q[4][:, :].rearrange("p (t v) -> p t v", t=NT),
                                       ACT.Copy).then_inc(s_vth, 1)
                    if k == 4 and g in G:
                        act.wait_ge(s_kt, g + 1)
                        for d in range(2):
                            act.activation(kh[:, d, :], q[2 + d][:, :], ACT.Copy).then_inc(s_kth, 1)
                        act.wait_ge(s_am, 3 * g + 3)
                        act.activation(ath[:, :], con[:, :], ACT.Copy).then_inc(s_ath, 1)
                    if 8 <= k <= 13 and g in G:
                        j = k - 8
                        d, t = STEPS[j]
                        m = 6 * g + j
                        act.wait_ge(s_con, m + 1)
                        if m:
                            act.wait_ge(s_st, m)
                        act.activation(con[:, :], q[4][:, :], ACT.Copy, scale=dif[:, d, t:t + 1]).then_inc(s_cs, 1)
                        act.wait_ge(s_st, m + 1)
                        if j >= 2:
                            act.wait_ge(s_in, m - 1)
                        nt = t + 1 if d == 0 else t - 1
                        act.activation(sth[:, d, :], st[:, d, :], ACT.Copy, scale=mid[:, d, nt:nt + 1])\
                           .then_inc(s_sth, 1)
                    if k == 11 and g in G:
                        for j in range(4):
                            act.wait_ge(*free_value(c, tile_of(g, 6 + j)))
                        act.activation(zs[:, :, :], zs[:, :, :], ACT.Silu).then_inc(s_z, 1)
                        act.preload_act_table_set(LN_EXP)

            @block.vector
            def _(dve):
                for n in range(first, first + 2):
                    split_lo(c, dve, n)
                for i, k in slots:
                    g, f = i, i - 1
                    pi, pk = before(i, k)
                    if (pi, pk) in plan and pk >= 10:
                        for j in range(2):
                            t, m = tile_of(pi, pk) + j, (pk - 10) * 2 + j
                            dve.wait_ge(c.tile_done, t + 1)
                            if pi > 1:
                                dve.wait_ge(*free_value(c, tile_of(pi - 1, pk) + j))
                            dve.tensor_tensor(c.h[:, m, :], c.h[:, m, :], bank(c, t)[:, :], ALU.add)\
                               .then_inc(c.bank_free[t % SB], 1)
                    if unit_in(i, k) is not None:
                        split_lo(c, dve, unit_in(i, k) + 2)
                    if k == 0 and f in G:
                        dve.wait_ge(s_rs, 2 * f + 2)
                        if f:
                            dve.wait_ge(s_ot, 2 * f)
                        for t in range(NT):
                            dve.tensor_scalar(o[:, t, :], q[t][:, :], rstd[:, t:t + 1], None, ALU.mult)\
                               .then_inc(s_on, 1)
                    if k in (1, 2) and f in G:
                        dve.wait_ge(s_ot, 2 * f + k)
                        dve.wait_ge(s_z, f + 1)
                        for j in (2 * k - 2, 2 * k - 1):
                            col = at["gla_onorm"] + j
                            dve.scalar_tensor_tensor(out=zs[:, j, :], in0=q[2 + j % 2][:, :],
                                                     scalar=par[:, col:col + 1], in1=zs[:, j, :], op0=ALU.mult,
                                                     op1=ALU.mult).then_inc(s_y, 1)
                    if k == 1 and g in G:
                        if g:
                            dve.wait_ge(s_e, 5 * g)
                        else:
                            dve.wait_ge(s_gl["go"], 3)
                        for d in range(2):
                            b = par[:, at["gla_b_gate"] + 4 * d + g:at["gla_b_gate"] + 4 * d + g + 1]
                            dve.wait_ge(s_act, 6 * g + 3 * d + 3)
                            dve.tensor_scalar(lg[:, d, :], q[d][:, :], b, 0.0, ALU.add, ALU.min).then_inc(s_lg, 1)
                            dve.wait_ge(s_lg, 6 * g + 3 * d + 1)
                            dve.tensor_tensor(lg[:, d, :], lg[:, d, :], em[:, d, :], ALU.subtract).then_inc(s_lg, 1)
                            dve.wait_ge(s_lg, 6 * g + 3 * d + 2)
                            v = (lambda b: b) if d == 0 else (lambda b: b[:, ::-1])
                            dve.tensor_tensor_scan(v(lg[:, d, :]), v(go[:, d, :]), v(lg[:, d, :]), 0.0, ALU.mult,
                                                   ALU.add).then_inc(s_lg, 1)
                        dve.wait_ge(s_lg, 6 * g + 6)
                        if g:
                            dve.wait_ge(s_sth, 6 * g)
                            dve.wait_ge(s_stl, 6 * g)
                        s4 = lg[:, :, :].rearrange("p d (t l) -> p d t l", t=NT)
                        for d in range(2):
                            dve.tensor_copy(mid[:, d, :], s4[:, d, :, P // 2 - 1 + d]).then_inc(s_small, 1)
                            dve.tensor_copy(tot[:, d, :], s4[:, d, :, (P - 1) * (1 - d)]).then_inc(s_small, 1)
                        dve.wait_ge(s_small, 4 * g + 4)
                        dve.tensor_tensor(dif[:, :, :], tot[:, :, :], mid[:, :, :], ALU.subtract).then_inc(s_cen, 1)
                        for d in range(2):
                            for u in range(2):
                                a = slice(u * T // 2, (u + 1) * T // 2)
                                dve.tensor_tensor(
                                    lg[:, d, a].rearrange("p (t l) -> p t l", t=2),
                                    lg[:, d, a].rearrange("p (t l) -> p t l", t=2),
                                    spread(mid[:, d, 2 * u:2 * u + 2], P), ALU.subtract).then_inc(s_cen, 1)
                    if k == 2 and g in G:
                        dve.wait_ge(s_e, 5 * g + 5)
                        dve.wait_ge(*free_value(c, tile_of(g, 0)))
                        dve.wait_ge(*free_value(c, tile_of(g, 1)))
                        for d in range(2):
                            dve.tensor_tensor(ep[:, d, :], ep[:, d, :], qs[:, :], ALU.mult).then_inc(s_g, 1)
                            dve.tensor_tensor(em[:, d, :], em[:, d, :], ks[:, :], ALU.mult).then_inc(s_g, 1)
                        dve.wait_ge(s_hi, 2 * g + 2)
                        for d in range(2):
                            dve.tensor_tensor(ql[:, d, :], ep[:, d, :], qh[:, d, :].bitcast(F32), ALU.subtract)\
                               .then_inc(s_lo, 1)
                            dve.tensor_tensor(kl[:, d, :], em[:, d, :], kh[:, d, :].bitcast(F32), ALU.subtract)\
                               .then_inc(s_lo, 1)
                    if k == 4 and f in G:
                        dve.wait_ge(s_yh, f + 1)
                        dve.tensor_tensor(yl[:, :, :], zs[:, :, :], yh[:, :, :].bitcast(F32), ALU.subtract)\
                           .then_inc(s_yl, 1)
                    if 4 <= k <= 7 and g in G:
                        j = k - 4
                        dve.wait_ge(s_vth, 4 * g + j + 1)
                        a = slice(j * P, (j + 1) * P)
                        dve.tensor_tensor(vl[:, :, a], q[4][:, :].rearrange("p (t v) -> p t v", t=NT),
                                          vh[:, :, a].bitcast(F32), ALU.subtract).then_inc(s_vtl, 1)
                    if k == 4 and g in G:
                        dve.wait_ge(s_kth, 2 * g + 2)
                        for d in range(2):
                            dve.tensor_tensor(kl[:, d, :], q[2 + d][:, :], kh[:, d, :].bitcast(F32), ALU.subtract)\
                               .then_inc(s_ktl, 1)
                        dve.wait_ge(s_att, g + 1)
                        if g == 0:
                            dve.wait_ge(s_zero, 1)
                        for d, mask in ((0, c.ge), (1, c.le)):
                            dve.copy_predicated(att[:, d, :].rearrange("p (t l) -> p t l", t=NT),
                                                again(mask[:, :].bitcast(I32), NT),
                                                q[d][:, :].rearrange("p (t l) -> p t l", t=NT)).then_inc(s_am, 1)
                        dve.wait_ge(s_am, 3 * g + 2)
                        if f in G:
                            dve.wait_ge(s_sq, 4 * f + 4)
                        dve.tensor_tensor(con[:, :], att[:, 0, :], att[:, 1, :], ALU.add).then_inc(s_am, 1)
                        dve.wait_ge(s_ath, g + 1)
                        dve.tensor_tensor(atl[:, :], con[:, :], ath[:, :].bitcast(F32), ALU.subtract)\
                           .then_inc(s_atl, 1)
                    if 8 <= k <= 13 and g in G:
                        j = k - 8
                        d, t = STEPS[j]
                        m = 6 * g + j
                        dve.wait_ge(s_cs, m + 1)
                        if j < 2:
                            dve.tensor_copy(st[:, d, :], con[:, :]).then_inc(s_st, 1)
                        else:
                            dve.scalar_tensor_tensor(out=st[:, d, :], in0=st[:, d, :], scalar=tot[:, d, t:t + 1],
                                                     in1=con[:, :], op0=ALU.mult, op1=ALU.add).then_inc(s_st, 1)
                        nt = t + 1 if d == 0 else t - 1
                        dve.wait_ge(s_sth, m + 1)
                        dve.wait_ge(s_st, m + 1)
                        dve.scalar_tensor_tensor(out=stl[:, d, :], in0=st[:, d, :], scalar=mid[:, d, nt:nt + 1],
                                                 in1=sth[:, d, :].bitcast(F32), op0=ALU.mult, op1=ALU.subtract)\
                           .then_inc(s_stl, 1)


CC = 512
CT = CC // P
CW = 31
PAD = CW - 1
MH = 8
QN, QR = 64, 32
QL, KL = 384, 256
MEM = 256
XH = 4
FF = 4096
P_ROW = [P * i * (i + 1) // 2 for i in range(NT)]
PT_ROUND = [[(0, 0)], [(1, 0), (3, 3 * P)], [(2, 0)]]
PT_AT = {0: 0, 1: T, 3: T + 3 * P, 2: 2 * T}
PT_SPAN = [(0, T), (T, 2 * T), (2 * T, 2 * T + 2 * P)]
P_COLS = 10 * P


def cols_of(w, a, n=P):
    return w[:, a:a + n].rearrange("(k p) m -> p k m", p=P)


def second_units(c, A):
    w_in, w_uq, w_ukv = A["w_in_2"][0], A["w_uq_2"][0], A["w_ukv_2"][0]
    kr = 2 * CC + QL + KL
    add_units(c, [cols_of(w_in, 2 * CC + P * j) for j in range(5)], 1)
    add_units(c, [[(0, cols_of(w_in, kr, 32)), (32, cols_of(w_in, kr, 32)), (64, cols_of(w_in, kr, 32)),
                   (96, cols_of(w_in, kr + 16, 16)), (112, cols_of(w_in, kr, 16))]], 1)
    add_units(c, [cols_of(w_in, P * (j // 2) + CC * (j % 2)) for j in range(8)], 1)
    add_units(c, [cols_of(w_in, kr + QR + P * j) for j in range(16)], 1)
    add_units(c, [[(QN * h, cols_of(w_ukv, (4 * j + h) * P + QN, QN)) for h in range(4)] for j in range(2)], 2)
    for h in range(MH):
        a = h * (QN + QR)
        add_units(c, [[(0, cols_of(w_uq, a, QN + QR)), (96, cols_of(w_uq, a + QN + 16, 16)),
                       (112, cols_of(w_uq, a + QN, 16))]], 1)
        add_units(c, [cols_of(w_ukv, h * P, QN)], 1, QN)
    add_units(c, [cols_of(A["w_mla_out_2"][0], 256 * m, 256) for m in range(4)], 2)
    add_units(c, [cols_of(A["w_conv_out_2"][0], 256 * m, 256) for m in range(4)], 2)
    add_units(c, [cols_of(A["w_out_2"][0], P * m) for m in range(KT)], 1)
    add_units(c, [cols_of(A["w_xq_2"][0], P * j) for j in range(XH)], 1)
    add_units(c, [cols_of(A["w_xkv_2"][0], P * j) for j in range(2 * XH)], 1)
    add_units(c, [cols_of(A["w_xo_2"][0], 256 * m, 256) for m in range(4)], 2)
    w1, w2 = A["w_mlp1_2"][0], A["w_mlp2_2"][0]
    for r in range(FF // D):
        add_units(c, [cols_of(w1, r * D + P * m) for m in range(KT)], 1)
        add_units(c, [cols_of(w2[r * D:(r + 1) * D, :], P * m) for m in range(KT)], 1)


def mix_project_stage(nc, c, A, cqh, cql, ckh, ckl, tbl, kth, ktl, z):
    par, at, q = c.par, c.at, c.q
    with ExitStack() as pre:
        pb = lambda n, s, d=F32: pre.enter_context(nc.sbuf_tensor("mixp_" + n, s, d))
        sem = stage_semaphores(nc, pre, "mixp_")
        lat = pb("latent", [P, 5, T])
        sq = pb("squares", [P, 5, T])
        rs = pb("latent_rstd", [P, 2, T])
        sig = pb("sigmoid", [P, 2, T])
        posi = pb("positions", [P, T], I32)
        ang = pb("angle", [P, T])
        trn = pb("turns", [P, T])
        cst = pb("rope_rows", [P, 3])
        krt = pb("key_rope", [P, T])
        join = pb("join", [P, P])
        n0 = c.next_unit
        N = 14
        c.next_unit = n0 + N
        s_fine = sem("refined")
        (s_p, s_sq, s_sum, s_rs, s_ln, s_lh, s_ll, s_tb, s_j, s_kh, s_kl, s_ta, s_jn) = (sem(n) for n in (
            "rope_loaded", "latent_squared", "latent_sums", "latent_rstd_s", "latent_normed", "latent_rounded",
            "latent_rest", "rope_steps", "key_joined", "key_rounded", "key_rest", "rope_sine", "join_ready"))
        tile = lambda k: c.tiles_before[n0 + k]
        with nc.Block() as block:
            @block.sync
            def _(sp):
                sp.dma_start(posi[:, :], A["positions_2"][0:1, :].broadcast_to([P, T])).then_inc(s_p, 16)
                sp.dma_start(cst[:, :], A["rope_rows"]).then_inc(s_p, 16)
                for n in range(n0, n0 + N + 2):
                    load_unit(c, sp, n)

            @block.gpsimd
            def _(pool):
                pool.memset(z[:, :, 0:PAD], 0.0).then_inc(s_jn, 1)
                pool.memset(join[:, :], 0.0).then_inc(s_jn, 1)
                for e, k0 in enumerate((64, 96)):
                    pool.wait_ge(s_jn, 2 + e)
                    pool.affine_select(out=join[:, :].rearrange("k (a b) -> k a b", a=4),
                                       in_=join[:, :].rearrange("k (a b) -> k a b", a=4),
                                       compare_op=ALU.not_equal, fill=1.0, base=-k0,
                                       pattern=[[0, 4], [-1, 32]], channel_multiplier=1).then_inc(s_jn, 1)

            @block.tensor
            def _(pe):
                for k in range(N + 1):
                    if k < N:
                        stream_products(c, pe, n0 + k, lambda j: c.uh[:, j, :], lambda j: c.ul[:, j, :])
                    if k in (4, 6):
                        e = (k - 4) // 2
                        pe.wait_ge(s_sq, (3, 5)[e])
                        for j in (range(3), range(3, 5))[e]:
                            last = pe.matmul(q[e][:, :], c.ones[:, :], sq[:, j, :], start=j in (0, 3),
                                             stop=j in (2, 4))
                        last.then_inc(s_sum, 1)
                    if k == 7:
                        pe.wait_ge(*free_value(c, tile(5)))
                        pe.wait_ge(s_jn, 4)
                        pe.matmul(q[2][:, :], join[:, :], krt[:, :], start=True, stop=True).then_inc(s_j, 1)

            @block.scalar
            def _(act):
                act.preload_act_table_set(LN_EXP)
                for n in range(n0, n0 + 2):
                    split_hi(c, act, n)
                for k in range(N + 1):
                    t = tile(k - 1) if k else None
                    if 1 <= k <= 5:
                        act.wait_ge(c.tile_done, t + 1)
                        act.activation(lat[:, k - 1, :], bank(c, t)[:, :], ACT.Copy)\
                           .then_inc(c.bank_free[t % SB], 1)
                        act.wait_ge(*free_value(c, t))
                        act.activation(sq[:, k - 1, :], lat[:, k - 1, :], ACT.Square).then_inc(s_sq, 1)
                    if k < N:
                        split_hi(c, act, n0 + k + 2)
                    if k in (5, 7):
                        e = (k - 5) // 2
                        act.wait_ge(s_sum, e + 1)
                        act.activation(rs[:, e, :], q[e][:, :], ACT.Ln, scale=1.0 / (QL, KL)[e],
                                       bias=c.eps[:, 0:1]).then_inc(s_rs, 1)
                        act.wait_ge(s_rs, 2 * e + 1)
                        act.activation(rs[:, e, :], rs[:, e, :], ACT.Exp, scale=-0.5).then_inc(s_rs, 1)
                        act.wait_ge(s_ln, (3, 5)[e])
                        if e == 0:
                            act.activation(cqh[:, :, :], lat[:, 0:3, :], ACT.Copy).then_inc(s_lh, 1)
                        else:
                            act.activation(ckh[:, :, :], lat[:, 3:5, :], ACT.Copy).then_inc(s_lh, 1)
                    if k == 5:
                        act.wait_ge(s_tb, 11)
                        act.activation(tbl[:, :], ang[:, :], ACT.Sin).then_inc(s_ta, 1)
                        act.preload_act_table_set(LN_EXP)
                    if k == 8:
                        act.wait_ge(s_j, 1)
                        act.activation(kth[64:P, :], q[2][64:P, :], ACT.Copy).then_inc(s_kh, 1)
                    if k >= 8 and k % 2 == 0:
                        e = (k - 8) // 2
                        act.wait_ge(c.tile_done, t + 1)
                        if e >= 2:
                            act.wait_ge(*free_value(c, tile(6 + 2 * (e - 2))))
                        act.activation(sig[:, e % 2, :], bank(c, t)[:, :], ACT.Sigmoid)\
                           .then_inc(c.bank_free[t % SB], 1)

            @block.vector
            def _(dve):
                for n in range(n0, n0 + 2):
                    split_lo(c, dve, n)
                TWO_PI = (6.28125, 0.0019350051879882812, 3.0199159819567e-07)
                dve.wait_ge(s_p, 32)
                dve.tensor_copy(ang[:, :], posi[:, :]).then_inc(s_tb, 1)
                dve.wait_ge(s_tb, 1)
                dve.tensor_scalar(ang[:, :], ang[:, :], cst[:, 0:1], None, ALU.mult).then_inc(s_tb, 1)
                dve.wait_ge(s_tb, 2)
                dve.tensor_scalar(trn[:, :], ang[:, :], 1.0 / 6.283185307179586, 12582912.0, ALU.mult, ALU.add)\
                   .then_inc(s_tb, 1)
                dve.wait_ge(s_tb, 3)
                dve.tensor_scalar(trn[:, :], trn[:, :], -12582912.0, None, ALU.add).then_inc(s_tb, 1)
                for j, part in enumerate(TWO_PI):
                    dve.wait_ge(s_tb, 4 + j)
                    dve.scalar_tensor_tensor(out=ang[:, :], in0=trn[:, :], scalar=-part, in1=ang[:, :],
                                             op0=ALU.mult, op1=ALU.add).then_inc(s_tb, 1)
                dve.wait_ge(s_tb, 7)
                dve.tensor_scalar(ang[:, :], ang[:, :], cst[:, 1:2], None, ALU.add).then_inc(s_tb, 1)
                dve.wait_ge(s_tb, 8)
                dve.tensor_scalar(trn[:, :], ang[:, :], 3.14159265, -6.283185307179586, ALU.is_gt, ALU.mult)\
                   .then_inc(s_tb, 1)
                dve.wait_ge(s_tb, 9)
                dve.tensor_tensor(ang[:, :], ang[:, :], trn[:, :], ALU.add).then_inc(s_tb, 1)
                dve.wait_ge(s_tb, 10)
                dve.tensor_scalar(ang[:, :], ang[:, :], 3.1415925, -3.1415925, ALU.min, ALU.max).then_inc(s_tb, 1)
                for k in range(N + 1):
                    t = tile(k - 1) if k else None
                    if k < N:
                        split_lo(c, dve, n0 + k + 2)
                    if k in (5, 7):
                        e = (k - 5) // 2
                        dve.wait_ge(s_rs, 2 * e + 2)
                        refine_rstd(dve, s_fine, 4 * e, rs[:, e, :], trn[:, :], q[e][:, :], (QL, KL)[e])
                        for j in (range(3), range(3, 5))[e]:
                            g = at["q_norm_g_2"] + j if e == 0 else at["kv_norm_g_2"] + j - 3
                            dve.scalar_tensor_tensor(out=lat[:, j, :], in0=lat[:, j, :], scalar=par[:, g:g + 1],
                                                     in1=rs[:, e, :], op0=ALU.mult, op1=ALU.mult)\
                               .then_inc(s_ln, 1)
                        dve.wait_ge(s_lh, e + 1)
                        lo, hi, src = ((cql, cqh, lat[:, 0:3, :]), (ckl, ckh, lat[:, 3:5, :]))[e]
                        dve.tensor_tensor(lo[:, :, :], src, hi[:, :, :].bitcast(F32), ALU.subtract)\
                           .then_inc(s_ll, 1)
                    if k == 6:
                        dve.wait_ge(s_ta, 1)
                        dve.tensor_scalar(tbl[:, :], tbl[:, :], cst[:, 2:3], None, ALU.mult).then_inc(s_tb, 1)
                        dve.wait_ge(s_tb, 12)
                        dve.wait_ge(c.tile_done, t + 1)
                        dve.tensor_tensor(krt[:, :], bank(c, t)[:, :], tbl[:, :], ALU.mult)\
                           .then_inc(c.bank_free[t % SB], 1)
                        dve.wait_ge(*free_value(c, t))
                        dve.tensor_scalar(tbl[:, :], tbl[:, :], float(QN + QR) ** -0.5, None, ALU.mult)\
                           .then_inc(s_tb, 1)
                    if k == 8:
                        dve.wait_ge(s_kh, 1)
                        dve.tensor_tensor(ktl[64:P, :], q[2][64:P, :], kth[64:P, :].bitcast(F32),
                                          ALU.subtract).then_inc(s_kl, 1)
                    if k >= 8 and k % 2 == 0:
                        e = (k - 8) // 2
                        dve.wait_ge(*free_value(c, t))
                        dve.tensor_tensor(z[:, e, PAD:], bank(c, t - 1)[:, :], sig[:, e % 2, :], ALU.mult)\
                           .then_inc(c.bank_free[(t - 1) % SB], 1)


def mix_gates_stage(nc, c, A, z, gates, acc):
    par, at = c.par, c.at
    n0 = c.next_unit
    N = 16
    c.next_unit = n0 + N
    LAST = CT - 1
    taps = [(m, k) for m in range(LAST) for k in range(CW)]
    share = -(-len(taps) // N)
    with ExitStack() as ctx:
        sem = stage_semaphores(nc, ctx, "gates_")
        s_tap, s_prod, s_add = sem("conv_taps"), sem("tap_products"), sem("taps_added")
        prod = ctx.enter_context(nc.sbuf_tensor("gates_tap_products", [P, 2, T], F32))
        with nc.Block() as block:
            @block.sync
            def _(sp):
                for n in range(n0, n0 + N + 2):
                    load_unit(c, sp, n)

            @block.tensor
            def _(pe):
                for k in range(N):
                    stream_products(c, pe, n0 + k, lambda j: c.uh[:, j, :], lambda j: c.ul[:, j, :])

            @block.scalar
            def _(act):
                for n in range(n0, n0 + 2):
                    split_hi(c, act, n)
                for k in range(N + 1):
                    if k < N:
                        split_hi(c, act, n0 + k + 2)
                    if k:
                        t = c.tiles_before[n0] + k - 1
                        act.wait_ge(c.tile_done, t + 1)
                        act.activation(gates[:, k - 1, :], bank(c, t)[:, :], ACT.Sigmoid)\
                           .then_inc(c.bank_free[t % SB], 1)
                    for e in range(2 * k, min(2 * k + 2, CW)):
                        w = par[:, at["conv_w_2"] + CT * e + LAST:at["conv_w_2"] + CT * e + LAST + 1]
                        src = z[:, LAST, e:e + T]
                        if e == 0:
                            b = par[:, at["conv_b_2"] + LAST:at["conv_b_2"] + LAST + 1]
                            act.activation(acc[:, LAST, :], src, ACT.Identity, scale=w, bias=b).then_inc(s_prod, 1)
                        else:
                            if e > 2:
                                act.wait_ge(s_add, e - 2)
                            act.activation(prod[:, e % 2, :], src, ACT.Copy, scale=w).then_inc(s_prod, 1)

            @block.gpsimd
            def _(pool):
                for e in range(1, CW):
                    pool.wait_ge(s_prod, e + 1)
                    if e > 1:
                        pool.wait_ge(s_add, e - 1)
                    pool.tensor_tensor(acc[:, LAST, :], acc[:, LAST, :], prod[:, e % 2, :], ALU.add)\
                        .then_inc(s_add, 1)

            @block.vector
            def _(dve):
                for n in range(n0, n0 + 2):
                    split_lo(c, dve, n)
                done = 0
                for s in range(N):
                    split_lo(c, dve, n0 + s + 2)
                    for m, k in taps[s * share:(s + 1) * share]:
                        w = at["conv_w_2"] + CT * k + m
                        b = at["conv_b_2"] + m
                        src = z[:, m, k:k + T]
                        if k == 0:
                            dve.tensor_scalar(acc[:, m, :], src, par[:, w:w + 1], par[:, b:b + 1], ALU.mult,
                                              ALU.add).then_inc(s_tap, 1)
                        else:
                            dve.wait_ge(s_tap, done)
                            dve.scalar_tensor_tensor(out=acc[:, m, :], in0=src, scalar=par[:, w:w + 1],
                                                     in1=acc[:, m, :], op0=ALU.mult, op1=ALU.add)\
                               .then_inc(s_tap, 1)
                        done += 1


def mix_attention_stage(nc, c, A, cqh, cql, ckh, ckl, tbl, kth, ktl):
    q = c.q
    with ExitStack() as ctx:
        sb = lambda n, s, d=F32: ctx.enter_context(nc.sbuf_tensor("att_" + n, s, d))
        sem = stage_semaphores(nc, ctx, "att_")
        vh, vl = sb("v_hi", [P, NT, MH * P], F32R), sb("v_lo", [P, NT, MH * P], F32R)
        qf = c.sq[:, 0, :]
        qth, qtl = sb("queries_hi", [P, T], F32R), sb("queries_lo", [P, T], F32R)
        pr = sb("p", [P, P_COLS])
        pth, ptl = sb("pt_hi", [P, P_COLS], F32R), sb("pt_lo", [P, P_COLS], F32R)
        neg = sb("minus_inf", [P, P], F32R)
        mx, sm = sb("row_max", [P, NT]), sb("row_sum", [P, NT])
        n0 = c.next_unit
        N = 2 + 2 * MH
        c.next_unit = n0 + N
        (s_neg, s_zero, s_vh, s_vl, s_qh, s_ql, s_kh, s_sc, s_mx, s_ex, s_rc, s_pn, s_pt, s_pth, s_ptl, s_pv, s_oh,
         s_ol) = (sem(n) for n in (
             "mask", "v_zeroed", "v_rounded", "v_rest", "q_rounded", "q_rest", "k_rounded", "scores", "row_max_s",
             "exps", "reciprocals", "normalised", "transposed", "pt_rounded", "pt_rest", "pv_done", "o_rounded",
             "o_rest"))
        tq = lambda h: c.tiles_before[n0 + 2 + 2 * h]
        SLOTS = MH + 2
        ROWS = [(3, 0, 0), (0, 1, 0), (2, 1, P), (1, 2, 0)]
        v_dst = lambda v, j, t: v[:, t, 4 * P * j:4 * P * (j + 1)].rearrange(
            "p (a e v) -> p a e v", a=2, e=4)[:, :, 0::3, :]
        v_src = lambda t, e: bank(c, t)[:, e * 4 * QN:(e + 1) * 4 * QN].rearrange("p (a e v) -> p a e v", a=2, e=2)
        with nc.Block() as block:
            @block.sync
            def _(sp):
                for n in range(n0, n0 + N + 2):
                    load_unit(c, sp, n)

            @block.gpsimd
            def _(pool):
                pool.memset(vh[:, :, :].bitcast(F32), 0.0).then_inc(s_zero, 1)
                pool.memset(vl[:, :, :].bitcast(F32), 0.0).then_inc(s_zero, 1)
                pool.memset(pr[:, 0:P], -1e30).then_inc(s_neg, 1)
                pool.wait_ge(s_neg, 1)
                pool.affine_select(out=neg[:, :], in_=pr[:, 0:P], compare_op=ALU.is_gt, fill=0.0, base=0,
                                   pattern=[[1, P]], channel_multiplier=-1).then_inc(s_neg, 1)

            @block.tensor
            def _(pe):
                for n in range(2):
                    hi, lo = w_view(c, n0 + n)
                    pe.wait_ge(c.w_split, n0 + n + 1)
                    for b in range(2):
                        t = c.tiles_before[n0 + n] + b
                        if t >= SB:
                            pe.wait_ge(c.bank_free[t % SB], t // SB)
                        for u in range(2):
                            a = slice((2 * b + u) * P, (2 * b + u + 1) * P)
                            for k in range(2):
                                last = mm3(pe, bank(c, t)[:, u * 4 * QN:(u + 1) * 4 * QN], ckh[:, k, a],
                                           ckl[:, k, a], hi[:, k, :], lo[:, k, :], k == 0, k == 1)
                        last.then_inc(c.tile_done, 1)
                for s in range(SLOTS):
                    f, g = s - 1, s - 2
                    if s < MH:
                        stream_products(c, pe, n0 + 2 + 2 * s, lambda j: cqh[:, j, :], lambda j: cql[:, j, :])
                    if 0 <= f < MH:
                        pe.wait_ge(s_ql, f + 1)
                        pe.wait_ge(*free_value(c, tq(f) + 1))
                        if f == 0:
                            pe.wait_ge(s_neg, 2)
                        if f:
                            pe.wait_ge(s_ex, 4 * f)
                        for r, (i, b, a) in enumerate(ROWS):
                            w, x = P * (i + 1), slice(i * P, (i + 1) * P)
                            mm3(pe, q[b][:, a:a + w], qth[:, x], qtl[:, x], kth[:, 0:w], ktl[:, 0:w], True, False)
                            last = pe.matmul(q[b][:, a + w - P:a + w], c.ident_r[:, :], neg[:, :], start=False,
                                             stop=True)
                            last.then_inc(s_sc, 1)
                    for r, blocks in enumerate(PT_ROUND):
                        if g >= 0:
                            pe.wait_ge(s_pn, 4 * g + 4)
                            if 3 * g + r:
                                pe.wait_ge(s_ptl, 3 * g + r)
                            for j, a in blocks:
                                for i in range(j, NT):
                                    b = a + (i - j) * P
                                    last = pe.transpose(q[3][:, b:b + P],
                                                        pr[:, P_ROW[i] + j * P:P_ROW[i] + (j + 1) * P],
                                                        c.ident[:, :])
                            last.then_inc(s_pt, 1)
                        if r == 0 and s < MH:
                            stream_products(c, pe, n0 + 3 + 2 * s, lambda j: ckh[:, j, :], lambda j: ckl[:, j, :])
                    if g >= 0:
                        if g == 0:
                            pe.wait_ge(s_vl, 4)
                            for t in range(c.tiles_before[n0], c.tiles_before[n0] + 4):
                                pe.wait_ge(*free_value(c, t))
                        if g % 2 == 0 and g:
                            pe.wait_ge(s_ol, g // 2)
                        v = slice(g * P, (g + 1) * P)
                        for j in range(NT):
                            pe.wait_ge(s_ptl, 3 * g + (1, 2, 3, 2)[j])
                            w = P * (NT - j)
                            a = slice(PT_AT[j], PT_AT[j] + w)
                            last = mm3(pe, q[4][:, j * P:T], vh[:, j, v], vl[:, j, v], pth[:, a], ptl[:, a],
                                       g % 2 == 0 and j == 0, g % 2 == 1 and j == NT - 1, True)
                        last.then_inc(s_pv, 1)

            @block.scalar
            def _(act):
                act.preload_act_table_set(LN_EXP)
                for n in range(n0, n0 + 2):
                    split_hi(c, act, n)
                act.wait_ge(s_zero, 2)
                for j in range(2):
                    split_hi(c, act, n0 + 2 + j)
                    for b in range(2):
                        t = c.tiles_before[n0] + 2 * j + b
                        act.wait_ge(c.tile_done, t + 1)
                        for e in range(2):
                            act.activation(v_dst(vh, j, 2 * b + e), v_src(t, e), ACT.Copy).then_inc(s_vh, 1)
                for s in range(SLOTS):
                    f, g = s - 1, s - 2
                    if s < MH:
                        split_hi(c, act, n0 + 4 + 2 * s)
                    if s < MH:
                        act.wait_ge(*free_value(c, tq(s)))
                        if s:
                            act.wait_ge(s_sc, 4 * s)
                        act.activation(qth[:, :], qf, ACT.Copy).then_inc(s_qh, 1)
                    if g >= 0:
                        act.wait_ge(s_pt, 3 * g + 1)
                        if g:
                            act.wait_ge(s_pv, g)
                        act.activation(pth[:, 0:T], q[3][:, :], ACT.Copy).then_inc(s_pth, 1)
                        for r in (1, 2):
                            act.wait_ge(s_pt, 3 * g + r + 1)
                            a, b = PT_SPAN[r]
                            act.activation(pth[:, a:b], q[3][:, 0:b - a], ACT.Copy).then_inc(s_pth, 1)
                    if 0 <= f < MH:
                        act.wait_ge(s_mx, 5 * f + 5)
                        if f == 0:
                            act.wait_ge(s_neg, 2)
                        if f:
                            act.wait_ge(s_pt, 3 * f)
                        for i, b, a in ROWS:
                            act.activation(pr[:, P_ROW[i]:P_ROW[i] + P * (i + 1)], q[b][:, a:a + P * (i + 1)],
                                           ACT.Exp, bias=mx[:, i:i + 1], accum_out=sm[:, i:i + 1])\
                               .then_inc(s_ex, 1)
                    if s < MH:
                        split_hi(c, act, n0 + 5 + 2 * s)
                    if s < MH:
                        t = tq(s) + 1
                        act.wait_ge(c.tile_done, t + 1)
                        act.activation(kth[0:QN, :], bank(c, t)[0:QN, :], ACT.Copy).then_inc(s_kh, 1)
                    if g >= 0 and g % 2 == 1:
                        act.wait_ge(s_pv, g + 1)
                        act.activation(c.uh[:, g // 2, :], q[4][:, :], ACT.Copy).then_inc(s_oh, 1)

            @block.vector
            def _(dve):
                for n in range(n0, n0 + 2):
                    split_lo(c, dve, n)
                for j in range(2):
                    split_lo(c, dve, n0 + 2 + j)
                    for b in range(2):
                        t = c.tiles_before[n0] + 2 * j + b
                        dve.wait_ge(s_vh, 4 * j + 2 * b + 2)
                        for e in range(2):
                            done, by = ((s_vl, 1), (c.bank_free[t % SB], 1))[e]
                            dve.tensor_tensor(v_dst(vl, j, 2 * b + e), v_src(t, e),
                                              v_dst(vh, j, 2 * b + e).bitcast(F32), ALU.subtract)\
                               .then_inc(done, by)
                for s in range(SLOTS):
                    f, g = s - 1, s - 2
                    if s < MH:
                        split_lo(c, dve, n0 + 4 + 2 * s)
                    if s < MH:
                        t = tq(s)
                        dve.wait_ge(c.tile_done, t + 1)
                        if s:
                            dve.wait_ge(s_ql, s)
                        dve.tensor_tensor(qf, bank(c, t)[:, :], tbl[:, :], ALU.mult)\
                           .then_inc(c.bank_free[t % SB], 1)
                    if 0 <= f < MH:
                        if f:
                            dve.wait_ge(s_ex, 4 * f)
                        for r, (i, b, a) in enumerate(ROWS):
                            dve.wait_ge(s_sc, 4 * f + (1, 3, 3, 4)[r])
                            dve.reduce_max(mx[:, i:i + 1], q[b][:, a:a + P * (i + 1)], AX.X).then_inc(s_mx, 1)
                        dve.wait_ge(s_mx, 5 * f + 4)
                        dve.tensor_scalar(mx[:, :], mx[:, :], -1.0, None, ALU.mult).then_inc(s_mx, 1)
                    if s < MH:
                        dve.wait_ge(s_qh, s + 1)
                        dve.tensor_tensor(qtl[:, :], qf, qth[:, :].bitcast(F32), ALU.subtract)\
                           .then_inc(s_ql, 1)
                    if g >= 0:
                        for r in range(3):
                            dve.wait_ge(s_pth, 3 * g + r + 1)
                            a, b = PT_SPAN[r]
                            dve.tensor_tensor(ptl[:, a:b], q[3][:, 0:b - a], pth[:, a:b].bitcast(F32),
                                              ALU.subtract).then_inc(s_ptl, 1)
                    if 0 <= f < MH:
                        dve.wait_ge(s_ex, 4 * f + 4)
                        dve.reciprocal(sm[:, :], sm[:, :]).then_inc(s_rc, 1)
                        dve.wait_ge(s_rc, f + 1)
                        for i in range(NT):
                            a = slice(P_ROW[i], P_ROW[i] + P * (i + 1))
                            dve.tensor_scalar(pr[:, a], pr[:, a], sm[:, i:i + 1], None, ALU.mult).then_inc(s_pn, 1)
                    if s < MH:
                        split_lo(c, dve, n0 + 5 + 2 * s)
                    if s < MH:
                        t = tq(s) + 1
                        dve.wait_ge(s_kh, s + 1)
                        dve.tensor_tensor(ktl[0:QN, :], bank(c, t)[0:QN, :], kth[0:QN, :].bitcast(F32),
                                          ALU.subtract).then_inc(c.bank_free[t % SB], 1)
                    if g >= 0 and g % 2 == 1:
                        dve.wait_ge(s_oh, g // 2 + 1)
                        dve.tensor_tensor(c.ul[:, g // 2, :], q[4][:, :], c.uh[:, g // 2, :].bitcast(F32),
                                          ALU.subtract).then_inc(s_ol, 1)


def merge_stage(nc, c, A, gates, acc, memh, meml):
    par, at, q = c.par, c.at, c.q
    with ExitStack() as ctx:
        sb = lambda n, s, d=F32: ctx.enter_context(nc.sbuf_tensor("merge_" + n, s, d))
        sem = stage_semaphores(nc, ctx, "merge_")
        sq = sb("conv_squares", [P, CT, T])
        rstd = sb("conv_rstd", [P, T])
        tmp = sb("newton", [P, T])
        mh, ml = sb("hi", [P, KT, T], F32R), sb("lo", [P, KT, T], F32R)
        s_mean, s_cen, s_sq, s_var, s_rs, s_fine, s_n, s_si, s_chi, s_clo, s_hi, s_lo, s_add = (sem(n) for n in (
            "mean", "centred", "squared", "variance", "rstd_s", "refined", "normed", "silu", "conv_rounded",
            "conv_rest", "rounded", "rest", "added"))
        MT = MEM // P
        rows = sb("mem_rows", [P, MT, D])
        mem_sq = sq[:, 0:2, :].rearrange("p a b -> p (a b)")
        ms, mem_rstd, mem_tmp = sb("mem_sum_sq", [P, MT]), sb("mem_rstd", [P, MT]), sb("mem_newton", [P, MT])
        s_min, s_msq, s_mrs, s_mfine, s_mn, s_mt, s_mhi, s_mlo = (sem("mem_" + n) for n in (
            "loaded", "squared", "rstd_s", "refined", "normed", "transposed", "rounded", "rest"))
        n0 = c.next_unit
        N = 8 + KT
        c.next_unit = n0 + N
        tile = lambda k: c.tiles_before[n0 + k]
        with nc.Block() as block:
            @block.sync
            def _(sp):
                sp.dma_start(rows[:, :, :], A["mem_2"][0].rearrange("(t p) d -> p t d", p=P)).then_inc(s_min, 16)
                for n in range(n0, n0 + N + 2):
                    load_unit(c, sp, n)

            @block.tensor
            def _(pe):
                for m in range(CT):
                    last = pe.matmul(q[0][:, :], c.ones[:, :], acc[:, m, :], start=m == 0, stop=m == CT - 1)
                last.then_inc(s_mean, 1)
                for k in range(N):
                    if k < 4:
                        stream_products(c, pe, n0 + k, lambda j: c.uh[:, j, :], lambda j: c.ul[:, j, :])
                    elif k < 8:
                        stream_products(c, pe, n0 + k, lambda j: c.uh[:, CT + j, :], lambda j: c.ul[:, CT + j, :],
                                        ready=(lambda j: (s_clo, j + 1)) if k == 4 else None)
                    else:
                        stream_products(c, pe, n0 + k, lambda j: mh[:, j, :], lambda j: ml[:, j, :],
                                        ready=(lambda j: (s_lo, j + 1)) if k == 8 else None)
                    if k == 0:
                        for m in range(CT):
                            pe.wait_ge(s_sq, m + 1)
                            last = pe.matmul(q[1][:, :], c.ones[:, :], sq[:, m, :], start=m == 0, stop=m == CT - 1)
                        last.then_inc(s_var, 1)
                    if k in (12, 13):
                        pe.wait_ge(s_mn, MT)
                        for m in range(4 * (k - 12), 4 * (k - 12) + 4):
                            if m >= 4:
                                pe.wait_ge(s_mlo, m - 3)
                            for t in range(MT):
                                last = pe.transpose(q[m % 4][:, t * P:(t + 1) * P], rows[:, t, m * P:(m + 1) * P],
                                                    c.ident[:, :])
                            last.then_inc(s_mt, 1)

            @block.scalar
            def _(act):
                act.preload_act_table_set(LN_EXP)
                for n in range(n0, n0 + 2):
                    split_hi(c, act, n)
                for k in range(N + 1):
                    if k < N:
                        split_hi(c, act, n0 + k + 2)
                    if k == 0:
                        for m in range(CT):
                            act.wait_ge(s_cen, m + 1)
                            act.activation(sq[:, m, :], acc[:, m, :], ACT.Square).then_inc(s_sq, 1)
                    if k == 1:
                        act.wait_ge(s_var, 1)
                        act.activation(rstd[:, :], q[1][:, :], ACT.Ln, scale=1.0 / CC, bias=c.eps[:, 0:1])\
                           .then_inc(s_rs, 1)
                        act.wait_ge(s_rs, 1)
                        act.activation(rstd[:, :], rstd[:, :], ACT.Exp, scale=-0.5).then_inc(s_rs, 1)
                    if k == 2:
                        for m in range(CT):
                            act.wait_ge(s_n, m + 1)
                            b = at["conv_ln_b_2"] + m
                            act.activation(acc[:, m, :], acc[:, m, :], ACT.Silu, bias=par[:, b:b + 1])\
                               .then_inc(s_si, 1)
                            act.wait_ge(s_si, m + 1)
                            act.activation(c.uh[:, CT + m, :], acc[:, m, :], ACT.Copy).then_inc(s_chi, 1)
                    if k == 9:
                        act.preload_act_table_set(LN_EXP)
                        act.wait_ge(s_min, 16)
                        act.wait_ge(s_var, 1)
                        for t in range(MT):
                            if t:
                                act.wait_ge(s_msq, t)
                            act.activation(mem_sq, rows[:, t, :], ACT.Square, accum_out=ms[:, t:t + 1])\
                               .then_inc(s_msq, 1)
                    if k == 10:
                        act.wait_ge(s_msq, MT)
                        act.activation(mem_rstd[:, :], ms[:, :], ACT.Ln, scale=1.0 / D, bias=c.eps[:, 0:1])\
                           .then_inc(s_mrs, 1)
                        act.wait_ge(s_mrs, 1)
                        act.activation(mem_rstd[:, :], mem_rstd[:, :], ACT.Exp, scale=-0.5).then_inc(s_mrs, 1)
                    if k in (13, 14):
                        for m in range(4 * (k - 13), 4 * (k - 13) + 4):
                            act.wait_ge(s_mt, m + 1)
                            g = at["norm_mem_g_2"] + m
                            act.activation(memh[:, m, :], q[m % 4][:, 0:MEM], ACT.Copy, scale=par[:, g:g + 1])\
                               .then_inc(s_mhi, 1)
                    if k > 8:
                        square_tile(c, act, k - 9, free_value(c, tile(k - 1)))
                    if 5 <= k <= 8:
                        for m in (2 * (k - 5), 2 * (k - 5) + 1):
                            act.wait_ge(s_add, m + 1)
                            act.activation(mh[:, m, :], gates[:, m, :], ACT.Copy).then_inc(s_hi, 1)

            @block.gpsimd
            def _(pool):
                for m in range(KT):
                    pool.wait_ge(*free_value(c, tile(m // 2) + m % 2))
                    pool.wait_ge(*free_value(c, tile(4 + m // 2) + m % 2))
                    pool.tensor_tensor(gates[:, m, :], gates[:, m, :], gates[:, KT + m, :], ALU.add)\
                        .then_inc(s_add, 1)
                add_squares(c, pool)

            @block.vector
            def _(dve):
                for n in range(n0, n0 + 2):
                    split_lo(c, dve, n)
                for k in range(N + 1):
                    if k < N:
                        split_lo(c, dve, n0 + k + 2)
                    if k == 0:
                        dve.wait_ge(s_mean, 1)
                        for m in range(CT):
                            dve.scalar_tensor_tensor(out=acc[:, m, :], in0=q[0][:, :], scalar=-1.0 / CC,
                                                     in1=acc[:, m, :], op0=ALU.mult, op1=ALU.add)\
                               .then_inc(s_cen, 1)
                    if 1 <= k <= 8:
                        for j in range(2):
                            t = tile(k - 1) + j
                            m = (k - 1) % 4 * 2 + j
                            dve.wait_ge(c.tile_done, t + 1)
                            x = m + (KT if k <= 4 else 0)
                            dve.tensor_tensor(gates[:, x, :], gates[:, x, :], bank(c, t)[:, :], ALU.mult)\
                               .then_inc(c.bank_free[t % SB], 1)
                    if k == 1:
                        dve.wait_ge(s_rs, 2)
                        dve.wait_ge(s_sq, CT)
                        refine_rstd(dve, s_fine, 0, rstd[:, :], tmp[:, :], q[1][:, :], CC)
                        for m in range(CT):
                            g = at["conv_ln_g_2"] + m
                            dve.wait_ge(s_cen, m + 1)
                            dve.scalar_tensor_tensor(out=acc[:, m, :], in0=acc[:, m, :], scalar=par[:, g:g + 1],
                                                     in1=rstd[:, :], op0=ALU.mult, op1=ALU.mult).then_inc(s_n, 1)
                    if k == 2:
                        for m in range(CT):
                            dve.wait_ge(s_chi, m + 1)
                            dve.tensor_tensor(c.ul[:, CT + m, :], acc[:, m, :], c.uh[:, CT + m, :].bitcast(F32),
                                              ALU.subtract).then_inc(s_clo, 1)
                    if 5 <= k <= 8:
                        for m in (2 * (k - 5), 2 * (k - 5) + 1):
                            dve.wait_ge(s_hi, m + 1)
                            dve.tensor_tensor(ml[:, m, :], gates[:, m, :], mh[:, m, :].bitcast(F32),
                                              ALU.subtract).then_inc(s_lo, 1)
                    if k == 11:
                        dve.wait_ge(s_mrs, 2)
                        refine_rstd(dve, s_mfine, 0, mem_rstd[:, :], mem_tmp[:, :], ms[:, :], D)
                        for t in range(MT):
                            dve.tensor_scalar(rows[:, t, :], rows[:, t, :], mem_rstd[:, t:t + 1], None, ALU.mult)\
                               .then_inc(s_mn, 1)
                    if k in (13, 14):
                        for m in range(4 * (k - 13), 4 * (k - 13) + 4):
                            g = at["norm_mem_g_2"] + m
                            dve.wait_ge(s_mhi, m + 1)
                            dve.scalar_tensor_tensor(out=meml[:, m, :], in0=q[m % 4][:, 0:MEM],
                                                     scalar=par[:, g:g + 1], in1=memh[:, m, :].bitcast(F32),
                                                     op0=ALU.mult, op1=ALU.subtract).then_inc(s_mlo, 1)
                    if k > 8:
                        t, m = tile(k - 1), k - 9
                        dve.wait_ge(c.tile_done, t + 1)
                        dve.tensor_tensor(c.h[:, m, :], c.h[:, m, :], bank(c, t)[:, :], ALU.add)\
                           .then_inc(c.bank_free[t % SB], 1)


def mix_and_cross_stages(nc, c, A, cross_norm):
    with ExitStack() as outer:
        ob = lambda n, s, d=F32: outer.enter_context(nc.sbuf_tensor("mix_" + n, s, d))
        gates = ob("gates", [P, 16, T])
        with ExitStack() as mid:
            mb = lambda n, s, d=F32: mid.enter_context(nc.sbuf_tensor("mix_" + n, s, d))
            acc = mb("conv", [P, CT, T])
            with ExitStack() as ctx:
                sb = lambda n, s, d=F32: ctx.enter_context(nc.sbuf_tensor("mix_" + n, s, d))
                cqh, cql = sb("cq_hi", [P, 3, T], F32R), sb("cq_lo", [P, 3, T], F32R)
                ckh, ckl = sb("ckv_hi", [P, 2, T], F32R), sb("ckv_lo", [P, 2, T], F32R)
                tbl = c.sumsq
                kth, ktl = sb("keys_hi", [P, T], F32R), sb("keys_lo", [P, T], F32R)
                with nc.sbuf_tensor("mix_z", [P, CT, PAD + T], F32) as z:
                    mix_project_stage(nc, c, A, cqh, cql, ckh, ckl, tbl, kth, ktl, z)
                    mix_gates_stage(nc, c, A, z, gates, acc)
                mix_attention_stage(nc, c, A, cqh, cql, ckh, ckl, tbl, kth, ktl)
            memh, meml = mb("mem_hi", [P, KT, MEM], F32R), mb("mem_lo", [P, KT, MEM], F32R)
            merge_stage(nc, c, A, gates, acc, memh, meml)
            cross_stage(nc, c, A, memh, meml, cross_norm)


def cross_project_stage(nc, c, A, memh, meml, kh, kl, vh, vl, qh, ql):
    N = 3 * XH
    n0 = c.next_unit
    c.next_unit = n0 + N
    scale = float(P) ** -0.5
    with ExitStack() as ctx:
        s_hi = stage_semaphores(nc, ctx, "xp_")("rounded")
        with nc.Block() as block:
            @block.sync
            def _(sp):
                for n in range(n0, n0 + N + 2):
                    load_unit(c, sp, n)

            @block.tensor
            def _(pe):
                for k in range(N):
                    if k < XH:
                        stream_products(c, pe, n0 + k, lambda j: c.uh[:, j, :], lambda j: c.ul[:, j, :])
                    elif k < 2 * XH:
                        stream_products(c, pe, n0 + k, lambda j: memh[:, j, :], lambda j: meml[:, j, :], MEM)
                    else:
                        n, t = n0 + k, c.tiles_before[n0 + k]
                        hi, lo = w_view(c, n)
                        pe.wait_ge(c.w_split, n + 1)
                        pe.wait_ge(c.bank_free[t % SB], t // SB)
                        for b in range(MEM // P):
                            a = slice(b * P, (b + 1) * P)
                            for j in range(KT):
                                last = mm3(pe, bank(c, t)[:, a], memh[:, j, a], meml[:, j, a], hi[:, j, :],
                                           lo[:, j, :], j == 0, j == KT - 1)
                        last.then_inc(c.tile_done, 1)

            def place(hi, lo, k):
                b = bank(c, c.tiles_before[n0 + k])
                if k < XH:
                    return hi[2][:, k, :], lo[2][:, k, :], b[:, :], scale
                if k < 2 * XH:
                    return hi[0][:, k - XH, :], lo[0][:, k - XH, :], b[:, 0:MEM], 1.0
                a = slice((k - 2 * XH) * P, (k - 2 * XH + 1) * P)
                return hi[1][:, :, a], lo[1][:, :, a], b[:, 0:MEM].rearrange("p (b v) -> p b v", v=P), 1.0

            @block.scalar
            def _(act):
                for n in range(n0, n0 + 2):
                    split_hi(c, act, n)
                for k in range(N + 1):
                    if k < N:
                        split_hi(c, act, n0 + k + 2)
                    if k:
                        dst, _, src, by = place((kh, vh, qh), (kl, vl, ql), k - 1)
                        act.wait_ge(c.tile_done, c.tiles_before[n0 + k - 1] + 1)
                        act.activation(dst, src, ACT.Copy, scale=by).then_inc(s_hi, 1)

            @block.vector
            def _(dve):
                for n in range(n0, n0 + 2):
                    split_lo(c, dve, n)
                for k in range(N + 1):
                    if k < N:
                        split_lo(c, dve, n0 + k + 2)
                    if k:
                        hi, lo, src, by = place((kh, vh, qh), (kl, vl, ql), k - 1)
                        dve.wait_ge(s_hi, k)
                        dve.scalar_tensor_tensor(out=lo, in0=src, scalar=by, in1=hi.bitcast(F32), op0=ALU.mult,
                                                 op1=ALU.subtract)\
                           .then_inc(c.bank_free[c.tiles_before[n0 + k - 1] % SB], 1)


def cross_attention_stage(nc, c, kh, kl, vh, vl, qh, ql):
    q = c.q
    MT = MEM // P
    with ExitStack() as ctx:
        sb = lambda n, s, d=F32: ctx.enter_context(nc.sbuf_tensor("xa_" + n, s, d))
        sem = stage_semaphores(nc, ctx, "xa_")
        pr = sb("p", [P, 2, NT, MEM])
        mx, sm = sb("row_max", [P, NT]), sb("row_sum", [P, NT])
        pth, ptl = sb("pt_hi", [P, MT, T], F32R), sb("pt_lo", [P, MT, T], F32R)
        s_sc, s_mx, s_ex, s_rc, s_pn, s_pt, s_pth, s_ptl, s_pv, s_oh, s_ol = (sem(n) for n in (
            "scores", "row_max_s", "exps", "reciprocals", "normalised", "transposed", "pt_rounded", "pt_rest",
            "pv_done", "o_rounded", "o_rest"))
        with nc.Block() as block:
            @block.tensor
            def _(pe):
                for s in range(XH + 1):
                    g = s - 1
                    if s < XH:
                        if s:
                            pe.wait_ge(s_ex, NT * s)
                        for i in range(NT):
                            a = slice(i * P, (i + 1) * P)
                            mm3(pe, q[i // 2][:, i % 2 * MEM:(i % 2 + 1) * MEM], qh[:, s, a], ql[:, s, a],
                                kh[:, s, :], kl[:, s, :], True, True).then_inc(s_sc, 1)
                    if g >= 0:
                        pe.wait_ge(s_pn, g + 1)
                        for b in range(MT):
                            if g:
                                pe.wait_ge(s_ptl, MT * (g - 1) + b + 1)
                            for i in range(NT):
                                last = pe.transpose(q[2 + b][:, i * P:(i + 1) * P],
                                                    pr[:, g % 2, i, b * P:(b + 1) * P], c.ident[:, :])
                            last.then_inc(s_pt, 1)
                        if g:
                            pe.wait_ge(s_ol, g)
                        for b in range(MT):
                            pe.wait_ge(s_ptl, MT * g + b + 1)
                            a = slice(g * P, (g + 1) * P)
                            last = mm3(pe, q[4][:, :], vh[:, b, a], vl[:, b, a], pth[:, b, :], ptl[:, b, :], b == 0,
                                       b == MT - 1)
                        last.then_inc(s_pv, 1)

            @block.scalar
            def _(act):
                act.preload_act_table_set(LN_EXP)
                for s in range(XH + 1):
                    g = s - 1
                    if g >= 0:
                        for b in range(MT):
                            act.wait_ge(s_pt, MT * g + b + 1)
                            if g:
                                act.wait_ge(s_pv, g)
                            act.activation(pth[:, b, :], q[2 + b][:, :], ACT.Copy).then_inc(s_pth, 1)
                    if s < XH:
                        act.wait_ge(s_mx, 5 * s + 5)
                        if s >= 2:
                            act.wait_ge(s_pt, MT * (s - 1))
                        for i in range(NT):
                            act.activation(pr[:, s % 2, i, :], q[i // 2][:, i % 2 * MEM:(i % 2 + 1) * MEM], ACT.Exp,
                                           bias=mx[:, i:i + 1], accum_out=sm[:, i:i + 1]).then_inc(s_ex, 1)
                    if g >= 0:
                        act.wait_ge(s_pv, g + 1)
                        act.activation(c.uh[:, g, :], q[4][:, :], ACT.Copy).then_inc(s_oh, 1)

            @block.vector
            def _(dve):
                for s in range(XH + 1):
                    g = s - 1
                    if s < XH:
                        if s:
                            dve.wait_ge(s_ex, NT * s)
                        for i in range(NT):
                            dve.wait_ge(s_sc, NT * s + i // 2 * 2 + 2)
                            dve.reduce_max(mx[:, i:i + 1], q[i // 2][:, i % 2 * MEM:(i % 2 + 1) * MEM], AX.X)\
                               .then_inc(s_mx, 1)
                        dve.wait_ge(s_mx, 5 * s + 4)
                        dve.tensor_scalar(mx[:, :], mx[:, :], -1.0, None, ALU.mult).then_inc(s_mx, 1)
                    if g >= 0:
                        for b in range(MT):
                            dve.wait_ge(s_pth, MT * g + b + 1)
                            dve.tensor_tensor(ptl[:, b, :], q[2 + b][:, :], pth[:, b, :].bitcast(F32), ALU.subtract)\
                               .then_inc(s_ptl, 1)
                    if s < XH:
                        dve.wait_ge(s_ex, NT * s + 4)
                        dve.reciprocal(sm[:, :], sm[:, :]).then_inc(s_rc, 1)
                        dve.wait_ge(s_rc, s + 1)
                        dve.tensor_tensor(pr[:, s % 2, :, :], pr[:, s % 2, :, :], spread(sm[:, :], MEM), ALU.mult)\
                           .then_inc(s_pn, 1)
                    if g >= 0:
                        dve.wait_ge(s_oh, g + 1)
                        dve.tensor_tensor(c.ul[:, g, :], q[4][:, :], c.uh[:, g, :].bitcast(F32), ALU.subtract)\
                           .then_inc(s_ol, 1)


def cross_out_stage(nc, c, A):
    n0 = c.next_unit
    N = 4
    c.next_unit = n0 + N
    with nc.Block() as block:
        @block.sync
        def _(sp):
            for n in range(n0, n0 + N + 2):
                load_unit(c, sp, n)

        @block.tensor
        def _(pe):
            for k in range(N):
                stream_products(c, pe, n0 + k, lambda j: c.uh[:, j, :], lambda j: c.ul[:, j, :])

        @block.scalar
        def _(act):
            for n in range(n0, n0 + 2):
                split_hi(c, act, n)
            for k in range(N + 1):
                if k < N:
                    split_hi(c, act, n0 + k + 2)
                if k:
                    for m in (2 * k - 2, 2 * k - 1):
                        square_tile(c, act, m, free_value(c, c.tiles_before[n0] + m))

        @block.gpsimd
        def _(pool):
            add_squares(c, pool)

        @block.vector
        def _(dve):
            for n in range(n0, n0 + 2):
                split_lo(c, dve, n)
            for k in range(N + 1):
                if k < N:
                    split_lo(c, dve, n0 + k + 2)
                if k:
                    for j in range(2):
                        m = 2 * (k - 1) + j
                        t = c.tiles_before[n0] + m
                        dve.wait_ge(c.tile_done, t + 1)
                        dve.tensor_tensor(c.h[:, m, :], c.h[:, m, :], bank(c, t)[:, :], ALU.add)\
                           .then_inc(c.bank_free[t % SB], 1)


def cross_stage(nc, c, A, memh, meml, norm):
    with ExitStack() as ctx:
        sb = lambda n, s, d=F32: ctx.enter_context(nc.sbuf_tensor("x_" + n, s, d))
        kh, kl = sb("k_hi", [P, XH, MEM], F32R), sb("k_lo", [P, XH, MEM], F32R)
        vh, vl = sb("v_hi", [P, MEM // P, XH * P], F32R), sb("v_lo", [P, MEM // P, XH * P], F32R)
        qh, ql = sb("q_hi", [P, XH, T], F32R), sb("q_lo", [P, XH, T], F32R)
        norm()
        cross_project_stage(nc, c, A, memh, meml, kh, kl, vh, vl, qh, ql)
        cross_attention_stage(nc, c, kh, kl, vh, vl, qh, ql)
        cross_out_stage(nc, c, A)


def mlp_stage(nc, c, A):
    CH = FF // D
    N = 2 * CH * KT
    n0 = c.next_unit
    c.next_unit = n0 + N
    with ExitStack() as ctx:
        sb = lambda n, s, d=F32: ctx.enter_context(nc.sbuf_tensor("mlp_" + n, s, d))
        sem = stage_semaphores(nc, ctx, "mlp_")
        r_ = sb("relu", [P, 2, T])
        sq = sb("squared", [P, 2, T])
        ah, al = sb("a_hi", [P, KT, T], F32R), sb("a_lo", [P, KT, T], F32R)
        s_sq, s_hi, s_lo = sem("squares"), sem("rounded"), sem("rest")
        tile = lambda k: c.tiles_before[n0 + k]
        with nc.Block() as block:
            @block.sync
            def _(sp):
                for n in range(n0, n0 + N + 2):
                    load_unit(c, sp, n)

            @block.tensor
            def _(pe):
                for k in range(N):
                    r, m = k // KT // 2, k % KT
                    if k // KT % 2 == 0:
                        stream_products(c, pe, n0 + k, lambda j: c.uh[:, j, :], lambda j: c.ul[:, j, :])
                    else:
                        stream_products(c, pe, n0 + k, lambda j: ah[:, j, :], lambda j: al[:, j, :],
                                        ready=(lambda j: (s_lo, KT * r + 1 + j)) if m == 0 else None)

            @block.scalar
            def _(act):
                for n in range(n0, n0 + 2):
                    split_hi(c, act, n)
                for k in range(N + 1):
                    if k < N:
                        split_hi(c, act, n0 + k + 2)
                    if k and (k - 1) // KT % 2 == 0:
                        r, m = (k - 1) // KT // 2, (k - 1) % KT
                        e = KT * r + m
                        t = tile(k - 1)
                        act.wait_ge(c.tile_done, t + 1)
                        if e >= 2:
                            act.wait_ge(s_sq, e - 1)
                        act.activation(r_[:, m % 2, :], bank(c, t)[:, :], ACT.Relu).then_inc(c.bank_free[t % SB], 1)
                        act.wait_ge(s_sq, e + 1)
                        if m == 0 and r:
                            act.wait_ge(c.tile_done, tile(2 * KT * r))
                        act.activation(ah[:, m, :], sq[:, m % 2, :], ACT.Copy).then_inc(s_hi, 1)
                    if k > N - KT:
                        square_tile(c, act, (k - 1) % KT, free_value(c, tile(k - 1)))

            @block.gpsimd
            def _(pool):
                add_squares(c, pool)

            @block.vector
            def _(dve):
                for n in range(n0, n0 + 2):
                    split_lo(c, dve, n)
                for k in range(N + 1):
                    if k and (k - 1) // KT % 2 == 0:
                        r, m = (k - 1) // KT // 2, (k - 1) % KT
                        e = KT * r + m
                        t = tile(k - 1)
                        dve.wait_ge(*free_value(c, t))
                        if e >= 2:
                            dve.wait_ge(s_lo, e - 1)
                        dve.tensor_tensor(sq[:, m % 2, :], r_[:, m % 2, :], r_[:, m % 2, :], ALU.mult)\
                           .then_inc(s_sq, 1)
                        if k < N:
                            split_lo(c, dve, n0 + k + 2)
                        dve.wait_ge(s_hi, e + 1)
                        dve.tensor_tensor(al[:, m, :], sq[:, m % 2, :], ah[:, m, :].bitcast(F32), ALU.subtract)\
                           .then_inc(s_lo, 1)
                    elif k:
                        m, t = (k - 1) % KT, tile(k - 1)
                        if k < N:
                            split_lo(c, dve, n0 + k + 2)
                        dve.wait_ge(c.tile_done, t + 1)
                        if k > 2 * KT:
                            dve.wait_ge(*free_value(c, tile(k - 1 - 2 * KT)))
                        dve.tensor_tensor(c.h[:, m, :], c.h[:, m, :], bank(c, t)[:, :], ALU.add)\
                           .then_inc(c.bank_free[t % SB], 1)
                    else:
                        split_lo(c, dve, n0 + k + 2)


def finish_stage(nc, c, out):
    with ExitStack() as ctx:
        sem = stage_semaphores(nc, ctx, "out_")
        rows = ctx.enter_context(nc.sbuf_tensor("out_rows", [P, NT, D], F32))
        s_t, s_a, s_v = sem("transposed"), sem("copied_act"), sem("copied_dve")
        o = out[0].rearrange("(t p) d -> p t d", p=P)
        with nc.Block() as block:
            @block.tensor
            def _(pe):
                for b in range(2 * NT):
                    if b >= 4:
                        pe.wait_ge((s_a, s_v)[b % 2], b // 2 - 1)
                    for j in range(4):
                        k = 4 * (b % 2) + j
                        last = pe.transpose(c.q[b % 4][:, j * P:(j + 1) * P],
                                            c.h[:, k, b // 2 * P:(b // 2 + 1) * P], c.ident[:, :])
                    last.then_inc(s_t, 1)

            @block.scalar
            def _(act):
                for t in range(NT):
                    act.wait_ge(s_t, 2 * t + 1)
                    act.activation(rows[:, t, 0:T], c.q[2 * t % 4][:, :], ACT.Copy).then_inc(s_a, 1)

            @block.vector
            def _(dve):
                for t in range(NT):
                    dve.wait_ge(s_t, 2 * t + 2)
                    dve.tensor_copy(rows[:, t, T:D], c.q[(2 * t + 1) % 4][:, :]).then_inc(s_v, 1)

            @block.sync
            def _(sp):
                for t in range(NT):
                    sp.wait_ge(s_a, t + 1)
                    sp.wait_ge(s_v, t + 1)
                    sp.dma_start(o[:, t, :], rows[:, t, :]).then_inc(c.stored, 16)
                sp.wait_ge(c.stored, 16 * NT)


def build(nc, A, out):
    c = Ctx()
    c.units, c.tiles_before, c.loaded, c.next_unit, c.arrived = [], [0], 0, 0, [0] * RAW
    c.hi_next, c.lo_next = 0, 0
    with ExitStack() as ctx:
        sb = lambda n, s, d=F32: ctx.enter_context(nc.sbuf_tensor(n, s, d))
        sem = lambda n: ctx.enter_context(nc.semaphore(n))
        c.stream = [ctx.enter_context(nc.psum_tensor(f"stream{j}", [P, T], F32)) for j in range(SB)]
        c.q = [ctx.enter_context(nc.psum_tensor(f"q{j}", [P, T], F32)) for j in range(8 - SB)]
        c.w_loaded = [sem(f"weights_loaded{j}") for j in range(RAW)]
        c.w_rounded, c.w_split, c.tile_done = sem("weights_rounded"), sem("weights_split"), sem("tile_done")
        c.square_ready, c.square_added = sem("square_ready"), sem("square_added")
        c.squared, c.added, c.streamed = 0, 0, 0
        c.stored = sem("output_stored")
        c.bank_free = [sem(f"bank_free{j}") for j in range(SB)]
        c.h = sb("h", [P, KT, T])
        c.uh, c.ul = sb("u_hi", [P, KT, T], F32R), sb("u_lo", [P, KT, T], F32R)
        c.raw = sb("weights_raw", [P, RAW, UNIT])
        c.w_hi, c.w_lo = sb("weights_hi", [P, WS, UNIT], F32R), sb("weights_lo", [P, WS, UNIT], F32R)
        c.ones, c.ident = sb("ones", [P, P]), sb("ident", [P, P])
        c.ge, c.le = sb("mask_ge", [P, P]), sb("mask_le", [P, P])
        c.gt_r, c.lt_r = sb("mask_gt", [P, P], F32R), sb("mask_lt", [P, P], F32R)
        c.ident_r = sb("ident_r", [P, P], F32R)
        c.eps = sb("eps", [P, 1])

        rows = lambda a: a.rearrange("(r p) -> r p", p=P)
        vectors = [
            ("ssd_conv_w", 160, A["ssd_conv_w"][0].rearrange("k (r p) -> (k r) p", p=P)),
            ("ssd_conv_b", 32, rows(A["ssd_conv_b"][0])),
            ("ssd_norm", 8, rows(A["ssd_norm"][0])),
            ("ssd_gnorm", 16, rows(A["ssd_gnorm"][0])),
            ("gla_norm", 8, rows(A["gla_norm"][0])),
            ("gla_b_gate", 8, A["gla_b_gate"][0].rearrange("a (r p) -> (a r) p", p=P)),
            ("gla_onorm", 4, rows(A["gla_onorm"][0])),
            ("conv_w_2", 124, A["conv_w_2"][0].rearrange("k (r p) -> (k r) p", p=P)),
            ("conv_b_2", 4, rows(A["conv_b_2"][0])),
            ("conv_ln_g_2", 4, rows(A["conv_ln_g_2"][0])),
            ("conv_ln_b_2", 4, rows(A["conv_ln_b_2"][0])),
            ("q_norm_g_2", 3, rows(A["q_norm_g_2"][0])),
            ("kv_norm_g_2", 2, rows(A["kv_norm_g_2"][0])),
            ("final_norm", 8, rows(A["final_norm"])),
            ("norm_mix_g_2", 8, rows(A["norm_mix_g_2"][0])),
            ("norm_xattn_g_2", 8, rows(A["norm_xattn_g_2"][0])),
            ("norm_mem_g_2", 8, rows(A["norm_mem_g_2"][0])),
            ("norm_mlp_g_2", 8, rows(A["norm_mlp_g_2"][0])),
            ("final_norm_g_2", 8, rows(A["final_norm_g_2"])),
        ]
        c.at, c.ptiles, c.prows, used = {}, [], [], 0
        for name, n, view in vectors:
            c.at[name] = used
            done = 0
            while done < n:
                if used % P == 0:
                    c.ptiles.append([])
                    c.prows.append(0)
                m = min(n - done, P - used % P)
                c.ptiles[-1].append((used % P, view[done:done + m]))
                c.prows[-1] = used % P + m
                done += m
                used += m
        c.at["ssd_d"] = len(c.ptiles) * P
        c.par = sb("params", [P, len(c.ptiles) * P + SH // 2])
        par, at = c.par, c.at
        col = lambda name: (lambda k: par[:, at[name] + k:at[name] + k + 1])

        ssd_plan, gla_plan = ssd_units(c, A), gla_units(c, A)
        second_units(c, A)
        start_stage(nc, c, A)
        hk = lambda k: c.h[:, k, :]
        uh, ul = (lambda k: c.uh[:, k, :]), (lambda k: c.ul[:, k, :])
        norm_stage(nc, c, "ssd_in", hk, KT, col("ssd_norm"), uh, ul)
        ssd_stage(nc, c, A, ssd_plan)
        c.sq, c.sumsq = sb("h_squares", [P, 2, T]), sb("h_sum_of_squares", [P, T])
        norm_stage(nc, c, "gla_in", hk, KT, col("gla_norm"), uh, ul)
        gla_stage(nc, c, A, gla_plan)

        norm_stage(nc, c, "first_out", hk, KT, col("final_norm"), None, None, plain=hk, summed=True,
                   sum_next=True)
        norm_stage(nc, c, "mix_in", hk, KT, col("norm_mix_g_2"), uh, ul, summed=True)
        mix_and_cross_stages(nc, c, A, lambda: norm_stage(nc, c, "cross_in", hk, KT, col("norm_xattn_g_2"), uh, ul,
                                                          summed=True))
        norm_stage(nc, c, "mlp_in", hk, KT, col("norm_mlp_g_2"), uh, ul, summed=True)
        mlp_stage(nc, c, A)
        norm_stage(nc, c, "last", hk, KT, col("final_norm_g_2"), None, None, plain=hk,
                   summed=True)
        finish_stage(nc, c, out)


def rope_rows():
    import numpy as np
    half = QR // 2
    row = np.arange(P)
    freq = np.float32(10000.0) ** (-np.arange(half, dtype=np.float32) / np.float32(half))
    t = np.zeros((P, 3), np.float32)
    t[:, 0] = np.where(row >= QN, freq[row % half], 0)
    t[:, 1] = np.where(row < QN + QR, np.pi / 2, 0)
    t[:, 2] = np.where((row >= QN + QR) & (row < QN + QR + half), -1, 1)
    return t


_INS = ["x", "ssd_norm", "ssd_w_in", "ssd_conv_w", "ssd_conv_b", "ssd_dt_bias", "ssd_a_log", "ssd_d", "ssd_gnorm",
        "ssd_w_out", "gla_norm", "gla_w_in", "gla_w_gate", "gla_b_gate", "gla_onorm", "gla_w_out", "final_norm",
        "mem_2", "positions_2", "norm_mix_g_2", "w_in_2", "conv_w_2", "conv_b_2", "conv_ln_g_2", "conv_ln_b_2",
        "w_conv_out_2", "q_norm_g_2", "w_uq_2", "kv_norm_g_2", "w_ukv_2", "w_mla_out_2", "w_out_2",
        "norm_xattn_g_2", "norm_mem_g_2", "w_xq_2", "w_xkv_2", "w_xo_2", "norm_mlp_g_2", "w_mlp1_2", "w_mlp2_2",
        "final_norm_g_2"]


def kernel(**inputs):
    import numpy as _np
    import concourse.bacc as _bacc
    from concourse import mybir as _mybir
    from concourse.bass_utils import run_bass_kernel_spmd as _run

    nc = _bacc.Bacc("TRN2", target_bir_lowering=False, num_devices=1)
    inputs["rope_rows"] = rope_rows()
    arrays, views = {}, {}
    for name in _INS + ["rope_rows"]:
        a = _np.ascontiguousarray(inputs[name])
        arrays[f"in_{name}_dram"] = a
        views[name] = nc.dram_tensor(f"in_{name}_dram", a.shape, _mybir.dt.from_np(a.dtype),
                                     kind="ExternalInput").ap()
    out = nc.dram_tensor("out_0_dram", (1, T, D), _mybir.dt.float32, kind="ExternalOutput").ap()
    build(nc, views, out)
    r = _run(nc, [arrays], core_ids=[0])
    return r.results[0]["out_0_dram"]
```
